# Optimizing a Trainium2 kernel written in Bass

```python
import math
import jax, jax.numpy as jnp
from jax import lax
import numpy as np

D_MODEL = 2048
BATCH = 1
SEQ = 256
DEPTH = 1

HEAD_DIM = 128
MOBA_HEADS = 6
NSA_HEADS = 6
NSA_KV_HEADS = 2
NSA_GROUP = NSA_HEADS // NSA_KV_HEADS
MEM_HEADS = 4
MEM_TOKENS = 256
MOBA_W = MOBA_HEADS * HEAD_DIM
NSA_W = NSA_HEADS * HEAD_DIM
NSA_KV_W = NSA_KV_HEADS * HEAD_DIM
MEM_W = MEM_HEADS * HEAD_DIM
MIX_W = MOBA_W + NSA_W + MEM_W
MOBA_BLOCK = 256
MOBA_TOPK = 3
NSA_CMP_LEN = 32
NSA_CMP_STRIDE = 16
NSA_CMP_HIDDEN = HEAD_DIM
NSA_SEL_BLOCK = 64
NSA_SEL_TOPK = 16
NSA_WINDOW = 512
NSA_N_BRANCH = 3
ROPE_THETA = 10000.0
LN_EPS = 1e-5
Q_CHUNK = 32
WIN_CHUNK = 128
NEG_INF = -1e30
FORCE_SCORE = 1e4
DN_ALPHA = (2.0 * DEPTH) ** 0.25
DN_BETA = (8.0 * DEPTH) ** -0.25
IN_SIZES = [MOBA_W, MOBA_W, MOBA_W, NSA_W, 6 * NSA_KV_W, NSA_N_BRANCH * NSA_HEADS, MEM_W, MIX_W]
IN_W = sum(IN_SIZES)

kernel_name = "hymba_moba_nsa_memory_deepnorm_layer"

def _masked_softmax(logits, mask):
    logits = jnp.where(mask, logits.astype(jnp.float32), NEG_INF)
    return jax.nn.softmax(logits, axis=-1)

def _rope(x, pos):
    half = HEAD_DIM // 2
    inv = ROPE_THETA ** (-jnp.arange(half, dtype=jnp.float32) / half)
    ang = pos.astype(jnp.float32)[..., None] * inv
    cos = jnp.cos(ang)[:, :, None, :]
    sin = jnp.sin(ang)[:, :, None, :]
    xf = x.astype(jnp.float32)
    x1, x2 = xf[..., :half], xf[..., half:]
    return jnp.concatenate([x1 * cos - x2 * sin, x1 * sin + x2 * cos], axis=-1).astype(x.dtype)

def _to_chunks(a, c):
    return a.reshape(a.shape[0], -1, c, *a.shape[2:]).swapaxes(0, 1)

def _from_chunks(o):
    o = o.swapaxes(0, 1)
    return o.reshape(o.shape[0], -1, *o.shape[3:])

def _layer_norm(y, gain, bias):
    yf = y.astype(jnp.float32)
    mu = jnp.mean(yf, axis=-1, keepdims=True)
    var = jnp.mean(jnp.square(yf - mu), axis=-1, keepdims=True)
    return ((yf - mu) * lax.rsqrt(var + LN_EPS) * gain.astype(jnp.float32) + bias.astype(jnp.float32)).astype(y.dtype)

def moba_attention(q, k, v):
    B, S, H, D = q.shape
    L = MOBA_BLOCK
    nb = -(-S // L)
    pad = nb * L - S
    kb = jnp.pad(k, ((0, 0), (0, pad), (0, 0), (0, 0))).reshape(B, nb, L, H, D)
    vb = jnp.pad(v, ((0, 0), (0, pad), (0, 0), (0, 0))).reshape(B, nb, L, H, D)
    k_mean = jnp.mean(kb.astype(jnp.float32), axis=2).astype(q.dtype)
    qpos = np.arange(S)
    qblk = qpos // L
    gate = jnp.einsum('bshd,bnhd->bshn', q, k_mean).astype(jnp.float32)
    past = np.arange(nb)[None, :] < qblk[:, None]
    gate = jnp.where(past[None, :, None, :], gate, NEG_INF)
    _, top_idx = lax.top_k(gate, min(MOBA_TOPK, nb))
    top_valid = top_idx < jnp.asarray(qblk)[None, :, None, None]
    own = jnp.broadcast_to(jnp.asarray(qblk, dtype=top_idx.dtype)[None, :, None, None], (B, S, H, 1))
    blk_idx = jnp.concatenate([top_idx, own], axis=-1)
    blk_valid = jnp.concatenate([top_valid, jnp.ones((B, S, H, 1), bool)], axis=-1)
    kb_t = kb.transpose(0, 3, 1, 2, 4)
    vb_t = vb.transpose(0, 3, 1, 2, 4)
    b_ix = jnp.arange(B)[:, None, None, None]
    h_ix = jnp.arange(H)[None, None, :, None]
    scale = HEAD_DIM ** -0.5

    def chunk(args):
        qc, ic, mc, pc = args
        kg = kb_t[b_ix, h_ix, ic]
        vg = vb_t[b_ix, h_ix, ic]
        s = jnp.einsum('bchd,bchjld->bchjl', qc, kg) * scale
        kpos = ic[..., None] * L + jnp.arange(L)
        mask = mc[..., None] & (kpos <= pc[None, :, None, None, None])
        Bc, C = qc.shape[0], qc.shape[1]
        p = _masked_softmax(s.reshape(Bc, C, H, -1), mask.reshape(Bc, C, H, -1))
        return jnp.einsum('bchn,bchnd->bchd', p.astype(vg.dtype), vg.reshape(Bc, C, H, -1, D))

    out = lax.map(chunk, (_to_chunks(q, Q_CHUNK), _to_chunks(blk_idx, Q_CHUNK),
                          _to_chunks(blk_valid, Q_CHUNK), jnp.arange(S).reshape(-1, Q_CHUNK)))
    return _from_chunks(out)

def _compress(kv, pos_emb, w1, w2):
    S = kv.shape[1]
    n_cmp = (S - NSA_CMP_LEN) // NSA_CMP_STRIDE + 1
    idx = np.arange(n_cmp)[:, None] * NSA_CMP_STRIDE + np.arange(NSA_CMP_LEN)[None, :]
    blocks = kv[:, idx] + pos_emb[None, None, :, None, :]
    hid = jax.nn.silu(jnp.einsum('bnlgd,lde->bnge', blocks, w1))
    return jnp.einsum('bnge,ed->bngd', hid, w2), idx

def nsa_attention(q, k_cmp, v_cmp, k_sel, v_sel, k_win, v_win, gates, pos,
                  cmp_pos_k, w_cmp1_k, w_cmp2_k, cmp_pos_v, w_cmp1_v, w_cmp2_v):
    B, S, H, D = q.shape
    G, R = NSA_KV_HEADS, NSA_GROUP
    scale = HEAD_DIM ** -0.5
    q_r = _rope(q, pos)
    qg = q.reshape(B, S, G, R, D)
    qg_r = q_r.reshape(B, S, G, R, D)
    qpos = np.arange(S)

    kc, idx = _compress(k_cmp, cmp_pos_k, w_cmp1_k, w_cmp2_k)
    vc, _ = _compress(v_cmp, cmp_pos_v, w_cmp1_v, w_cmp2_v)
    n_cmp = idx.shape[0]
    cmp_mask = idx[None, :, -1] <= qpos[:, None]
    s_c = jnp.einsum('bsgrd,bngd->bsgrn', qg, kc) * scale
    p_c = _masked_softmax(s_c, cmp_mask[None, :, None, None, :]) * cmp_mask[None, :, None, None, :]
    o_cmp = jnp.einsum('bsgrn,bngd->bsgrd', p_c.astype(vc.dtype), vc)

    SB = NSA_SEL_BLOCK
    n_sel = S // SB
    c_start = np.arange(n_cmp) * NSA_CMP_STRIDE
    s_start = np.arange(n_sel) * SB
    overlap = np.clip(np.minimum(c_start[:, None] + NSA_CMP_LEN, s_start[None, :] + SB)
                      - np.maximum(c_start[:, None], s_start[None, :]), 0, None) / NSA_CMP_LEN
    agg = jnp.asarray(overlap, dtype=jnp.float32)
    p_slc = jnp.einsum('bsgrn,nj->bsgj', p_c, agg)
    cur = qpos // SB
    j = np.arange(n_sel)
    causal = j[None, :] <= cur[:, None]
    forced = causal & ((j[None, :] == 0) | (j[None, :] >= cur[:, None] - 1))
    score = jnp.where(forced[None, :, None, :], FORCE_SCORE,
                      jnp.where(causal[None, :, None, :], p_slc, -1.0))
    _, sel_idx = lax.top_k(score, min(NSA_SEL_TOPK, n_sel))
    sel_valid = sel_idx <= jnp.asarray(cur)[None, :, None, None]
    ks_t = k_sel.reshape(B, n_sel, SB, G, D).transpose(0, 3, 1, 2, 4)
    vs_t = v_sel.reshape(B, n_sel, SB, G, D).transpose(0, 3, 1, 2, 4)
    b_ix = jnp.arange(B)[:, None, None, None]
    g_ix = jnp.arange(G)[None, None, :, None]

    def chunk(args):
        qc, ic, mc, pc = args
        kg = ks_t[b_ix, g_ix, ic]
        vg = vs_t[b_ix, g_ix, ic]
        s = jnp.einsum('bcgrd,bcgjld->bcgrjl', qc, kg) * scale
        kpos = ic[..., None] * SB + jnp.arange(SB)
        mask = mc[..., None] & (kpos <= pc[None, :, None, None, None])
        Bc, C = qc.shape[0], qc.shape[1]
        p = _masked_softmax(s.reshape(Bc, C, G, R, -1), mask.reshape(Bc, C, G, 1, -1))
        return jnp.einsum('bcgrn,bcgnd->bcgrd', p.astype(vg.dtype), vg.reshape(Bc, C, G, -1, D))

    o_sel = _from_chunks(lax.map(chunk, (_to_chunks(qg_r, Q_CHUNK), _to_chunks(sel_idx, Q_CHUNK),
                                         _to_chunks(sel_valid, Q_CHUNK), jnp.arange(S).reshape(-1, Q_CHUNK))))

    W, C = NSA_WINDOW, WIN_CHUNK
    nw = S // C
    k_w = _rope(k_win, pos)
    kp = jnp.pad(k_w, ((0, 0), (W, 0), (0, 0), (0, 0)))
    vp = jnp.pad(v_win, ((0, 0), (W, 0), (0, 0), (0, 0)))
    widx = np.arange(nw)[:, None] * C + np.arange(C + W)[None, :]
    kw, vw = kp[:, widx], vp[:, widx]
    qw = qg_r.reshape(B, nw, C, G, R, D)
    s_w = jnp.einsum('bnqgrd,bnkgd->bnqgrk', qw, kw) * scale
    kpos = widx - W
    diff = qpos.reshape(nw, C)[:, :, None] - kpos[:, None, :]
    wmask = (kpos[:, None, :] >= 0) & (diff >= 0) & (diff < W)
    p_w = _masked_softmax(s_w, wmask[None, :, :, None, None, :])
    o_win = jnp.einsum('bnqgrk,bnkgd->bnqgrd', p_w.astype(vw.dtype), vw).reshape(B, S, G, R, D)

    g = jax.nn.sigmoid(gates.astype(jnp.float32)).reshape(B, S, G, R, NSA_N_BRANCH, 1)
    o = (g[..., 0, :] * o_cmp.astype(jnp.float32) + g[..., 1, :] * o_sel.astype(jnp.float32)
         + g[..., 2, :] * o_win.astype(jnp.float32))
    return o.astype(q.dtype).reshape(B, S, H, D)

def memory_attention(q, mem, w_mem_kv):
    B, M = mem.shape[0], mem.shape[1]
    kv = jnp.einsum('bmd,de->bme', mem, w_mem_kv).reshape(B, M, 2, MEM_HEADS, HEAD_DIM)
    k, v = kv[:, :, 0], kv[:, :, 1]
    s = jnp.einsum('bshd,bmhd->bshm', q, k).astype(jnp.float32) * (HEAD_DIM ** -0.5)
    p = jax.nn.softmax(s, axis=-1)
    return jnp.einsum('bshm,bmhd->bshd', p.astype(v.dtype), v)

def setup_inputs(seed: int = 0) -> dict:
    key = jax.random.key(seed)
    ks = jax.random.split(key, 16)
    f = jnp.float32
    x = jax.random.normal(ks[0], (BATCH, SEQ, D_MODEL), f)
    mem = jax.random.normal(ks[1], (BATCH, MEM_TOKENS, D_MODEL), f)
    positions = jnp.broadcast_to(jnp.arange(SEQ, dtype=jnp.int32)[None, :], (BATCH, SEQ))
    w_in = jax.random.normal(ks[2], (D_MODEL, IN_W), f) * D_MODEL ** -0.5
    cmp_pos_k = jax.random.normal(ks[3], (NSA_CMP_LEN, HEAD_DIM), f) * 0.1
    w_cmp1_k = jax.random.normal(ks[4], (NSA_CMP_LEN, HEAD_DIM, NSA_CMP_HIDDEN), f) * (NSA_CMP_LEN * HEAD_DIM) ** -0.5
    w_cmp2_k = jax.random.normal(ks[5], (NSA_CMP_HIDDEN, HEAD_DIM), f) * NSA_CMP_HIDDEN ** -0.5
    cmp_pos_v = jax.random.normal(ks[6], (NSA_CMP_LEN, HEAD_DIM), f) * 0.1
    w_cmp1_v = jax.random.normal(ks[7], (NSA_CMP_LEN, HEAD_DIM, NSA_CMP_HIDDEN), f) * (NSA_CMP_LEN * HEAD_DIM) ** -0.5
    w_cmp2_v = jax.random.normal(ks[8], (NSA_CMP_HIDDEN, HEAD_DIM), f) * NSA_CMP_HIDDEN ** -0.5
    w_mem_kv = jax.random.normal(ks[9], (D_MODEL, 2 * MEM_W), f) * D_MODEL ** -0.5
    w_out = jax.random.normal(ks[10], (MIX_W, D_MODEL), f) * (MIX_W ** -0.5) * DN_BETA
    ln_gain = 1.0 + 0.02 * jax.random.normal(ks[11], (D_MODEL,), f)
    ln_bias = 0.02 * jax.random.normal(ks[12], (D_MODEL,), f)
    return {"x": x, "mem": mem, "positions": positions, "w_in": w_in,
            "cmp_pos_k": cmp_pos_k, "w_cmp1_k": w_cmp1_k, "w_cmp2_k": w_cmp2_k,
            "cmp_pos_v": cmp_pos_v, "w_cmp1_v": w_cmp1_v, "w_cmp2_v": w_cmp2_v,
            "w_mem_kv": w_mem_kv, "w_out": w_out, "ln_gain": ln_gain, "ln_bias": ln_bias}

def reference(x, mem, positions, w_in, cmp_pos_k, w_cmp1_k, w_cmp2_k, cmp_pos_v, w_cmp1_v, w_cmp2_v,
              w_mem_kv, w_out, ln_gain, ln_bias):
    B, S, _ = x.shape
    D = HEAD_DIM
    offsets = [int(o) for o in np.cumsum(IN_SIZES)[:-1]]
    for _layer in range(DEPTH):
        proj = jnp.einsum('bsd,de->bse', x, w_in)
        q_m, k_m, v_m, q_n, kv_n, g_n, q_mem, z = jnp.split(proj, offsets, axis=-1)
        q_m = _rope(q_m.reshape(B, S, MOBA_HEADS, D), positions)
        k_m = _rope(k_m.reshape(B, S, MOBA_HEADS, D), positions)
        v_m = v_m.reshape(B, S, MOBA_HEADS, D)
        o_m = moba_attention(q_m, k_m, v_m)
        kv_n = kv_n.reshape(B, S, 6, NSA_KV_HEADS, D)
        k_s_r = _rope(kv_n[:, :, 2], positions)
        o_n = nsa_attention(q_n.reshape(B, S, NSA_HEADS, D), kv_n[:, :, 0], kv_n[:, :, 1],
                            k_s_r, kv_n[:, :, 3], kv_n[:, :, 4], kv_n[:, :, 5],
                            g_n.reshape(B, S, NSA_HEADS, NSA_N_BRANCH), positions,
                            cmp_pos_k, w_cmp1_k, w_cmp2_k, cmp_pos_v, w_cmp1_v, w_cmp2_v)
        o_mem = memory_attention(q_mem.reshape(B, S, MEM_HEADS, D), mem, w_mem_kv)
        heads = jnp.concatenate([o_m.reshape(B, S, MOBA_W), o_n.reshape(B, S, NSA_W),
                                 o_mem.reshape(B, S, MEM_W)], axis=-1)
        gated = heads * jax.nn.silu(z)
        y = jnp.einsum('bse,ed->bsd', gated, w_out)
        x = _layer_norm(DN_ALPHA * x + y, ln_gain, ln_bias)
    return x


_drawn_inputs = setup_inputs


def setup_inputs(seed=0):
    import zlib

    import numpy as np

    out = dict(_drawn_inputs(seed))
    spreads = {}
    factors = {'mem': 3.774,
     'cmp_pos_k': 84.201,
     'w_cmp1_k': 6.339,
     'w_cmp2_k': 16.571,
     'cmp_pos_v': 21.467,
     'w_mem_kv': 3.714,
     'ln_gain': 24.495,
     'ln_bias': 24.537}
    for name, (base, spread) in spreads.items():
        noise = np.random.default_rng([zlib.crc32(name.encode()), seed]).standard_normal(out[name].shape)
        drawn = base * np.exp(spread * noise) if base else spread * noise
        out[name] = __import__('jax').numpy.asarray(drawn.astype(out[name].dtype))
    for name, factor in factors.items():
        out[name] = (out[name] * factor).astype(out[name].dtype)
    return out
```

```python
from contextlib import ExitStack

import concourse.bass as bass
from concourse import mybir
from concourse.alu_op_type import AluOpType as ALU

F32 = mybir.dt.float32
F32R = mybir.dt.float32r
I32 = mybir.dt.int32
ACT = mybir.ActivationFunctionType
AX_X = mybir.AxisListType.X

P = 128
S = 256
T = S // P
D = 2048
KT = D // P
COLS = 512
HEADS = 6
GROUP = 3
BRANCHES = 3
MEM_HEADS = 4
N_CMP = (S - 32) // 16 + 1
CMP_LEN = 32
CMP_STRIDE = 16
PIECE_KT = 2
PIECES = KT // PIECE_KT
RING = 4
SCALE = float(P) ** -0.5
ALPHA = 2.0 ** 0.25
EPS = 1e-5

MEM_K, MEM_V, Q_MEM, KV_CMP, KV_SEL, KV_WIN, HEAD0 = range(7)
Z0 = HEAD0 + HEADS
OUT0 = Z0 + D // COLS
SLABS = OUT0 + D // COLS

C_MASK = 0
C_CMASK = C_MASK + 3 * P
C_NONE = C_CMASK + 16 * T
C_ID = C_NONE + T
C_INV = C_ID + P
C_ALL = C_INV + P // 2

TWO_PI = (201 / 2 ** 5, 253 / 2 ** 17, 170 / 2 ** 25, 3.968374e-09)
PI_BELOW = 3.1415925
ROUND = 12582912.0

G_MEMK, G_QMEM, G_CMP, G_SEL, G_WIN, G_HEAD = 0, 2, 4, 6, 7, 8
G_Z = G_HEAD + 2 * HEADS

U_HEAD = MEM_HEADS
UNITS = U_HEAD + 4 * HEADS


class Count:

    def __init__(self, engine, semaphore):
        self.engine, self.semaphore, self.base, self.n = engine, semaphore, 0, 0

    def mark(self, instruction):
        instruction.then_inc(self.semaphore, 1)
        self.n += 1

    def wait(self):
        self.engine.wait_ge(self.semaphore, self.base + self.n)

    def loop(self, turn, per_turn):
        self.entry, self.per_turn = self.base + self.n, per_turn
        self.base, self.n = self.entry + turn * per_turn, 0

    def end_loop(self, turns):
        assert self.n == self.per_turn, self.n
        self.base, self.n = self.entry + turns * self.per_turn, 0


def build(nc, w, x_t, mem_t, x, w_gate, positions, consts, cmp_pos, w1_k, w1_v, w2, gain, bias, out):
    with ExitStack() as ctx:
        def sb(name, shape, dt=F32):
            return ctx.enter_context(nc.sbuf_tensor(name, shape, dt))

        def bank(name):
            return ctx.enter_context(nc.psum_tensor(name, [P, 512], F32))

        def sem(name):
            return ctx.enter_context(nc.semaphore(name))

        raw = sb("raw", [P, RING, PIECE_KT, COLS])
        split = sb("split", [P, RING, 2, PIECE_KT, COLS], F32R)
        x_hl = sb("x_hl", [P, 2, KT, S], F32R)
        b_hl = sb("b_hl", [P, 2, KT, S], F32R)
        area_a = sb("area_a", [P, KT * S])
        area_b = sb("area_b", [P, KT * S])
        x_raw = area_a[:].rearrange("p (k t) -> p k t", k=KT)
        w1k = area_a[:].rearrange("p (l e) -> p l e", l=CMP_LEN)
        heads = area_a[:].rearrange("p (t c) -> p t c", t=T)
        gain_sb, bias_sb = area_a[:, 0:D], area_a[:, D:2 * D]
        mem_raw = area_b[:].rearrange("p (k t) -> p k t", k=KT)
        w1v = area_b[:].rearrange("p (l e) -> p l e", l=CMP_LEN)
        res = area_b[:].rearrange("p (t c) -> p t c", t=T)

        nat = sb("nat", [P, T, COLS])
        rot = sb("rot", [P, T, 3, P])
        turned = sb("turned", [P, T, 3, P])
        head_t = sb("head_t", [P, 4, S])
        cmp_t = head_t
        nsa_k_t = sb("nsa_k_t", [P, 2, 2, S])
        nsa_v = sb("nsa_v", [P, 2, T, 2, P])
        mem_k_t = sb("mem_k_t", [P, MEM_HEADS, S])
        mem_q_t = sb("mem_q_t", [P, MEM_HEADS, S])
        mem_v = sb("mem_v", [P, T, MEM_HEADS, P])
        area_c = sb("area_c", [P, 2048])
        blocks = area_c[:, 0:2 * CMP_LEN * 2 * N_CMP].rearrange("p (w l g n) -> p w l g n", w=2, l=CMP_LEN, g=2)
        tanh_z = area_c[:, 0:1024].rearrange("p (t c) -> p t c", t=T)
        gated = area_c[:, 1024:2048].rearrange("p (t c) -> p t c", t=T)
        probs = sb("probs", [P, 2, COLS])
        probs_t = sb("probs_t", [P, 2, COLS])
        cs = sb("cs", [P, T, P])
        sn = sb("sn", [P, T, P])
        angle = probs_t[:, 0, 0:S].rearrange("p (t c) -> p t c", t=T)
        turns = probs_t[:, 1, 0:S].rearrange("p (t c) -> p t c", t=T)
        con = sb("con", [P, C_ALL])
        mask, ident = con[:, C_MASK:C_MASK + 3 * P], con[:, C_ID:C_ID + P]
        no_block = con[:, C_NONE:C_NONE + T]
        pos_i = sb("pos_i", [P, T], I32)
        pos_f = sb("pos_f", [P, T])
        cpos = sb("cpos", [P, 2, CMP_LEN])
        w2_sb = sb("w2_sb", [P, 2, P])
        hid = sb("hid", [P, 2, 2 * N_CMP])
        hid_in = sb("hid_in", [P, 2, 2 * N_CMP])
        hid_tanh = sb("hid_tanh", [P, 2, 2 * N_CMP])
        cmp_k_t = sb("cmp_k_t", [P, 2, N_CMP])
        cmp_v = sb("cmp_v", [N_CMP, 2, P])
        wg_raw = sb("wg_raw", [P, KT, HEADS * BRANCHES])
        wg_hl = sb("wg_hl", [P, 2, KT, HEADS * BRANCHES], F32R)
        gates = sb("gates", [P, T, HEADS * BRANCHES])
        waiter = sb("waiter", [P, 1])
        top = sb("top", [P, 2, T])
        shift = sb("shift", [P, 2, T])
        total = sb("total", [P, 2, T])
        weight = sb("weight", [P, 2, T])
        stats = sb("stats", [P, T, 4, 6])
        moments = sb("moments", [P, T, 2])
        rstd = sb("rstd", [P, T])
        power = sb("power", [P, T])
        centre = sb("centre", [P, T])

        acc = [bank(f"acc{t}") for t in range(T)]
        score = [bank(f"score{e}") for e in range(2)]
        xpose = [bank(f"xpose{e}") for e in range(2)]
        mixed = [bank(f"mixed{e}") for e in range(2)]

        w_landed = [sem(f"w_landed{i}") for i in range(RING)]
        mem_landed = [sem(f"mem_landed{i}") for i in range(4)]
        x_landed = sem("x_landed")
        con_landed = sem("con_landed")
        w1_landed = sem("w1_landed")
        res_landed = sem("res_landed")
        affine_landed = sem("affine_landed")
        out_landed = sem("out_landed")
        hi_ready = sem("hi_ready")
        lo_ready = sem("lo_ready")
        piece_used = sem("piece_used")
        first_done = sem("first_done")
        acc_free = sem("acc_free")
        y_free = sem("y_free")
        stat_hi = sem("stat_hi")
        stat_lo = sem("stat_lo")
        wg_hi = sem("wg_hi")
        wg_lo = sem("wg_lo")
        gates_done = sem("gates_done")
        gates_tanh = sem("gates_tanh")
        gates_ready = sem("gates_ready")
        reduced = sem("reduced")
        sines = sem("sines")
        roped = sem("roped")
        xpose_done = sem("xpose_done")
        xpose_out = sem("xpose_out")
        blocks_ready = sem("blocks_ready")
        hid_done = sem("hid_done")
        hid_taken = sem("hid_taken")
        hid_ready = sem("hid_ready")
        cmp_done = sem("cmp_done")
        cmp_ready = sem("cmp_ready")
        scores_done = sem("scores_done")
        max_ready = sem("max_ready")
        probs_ready = sem("probs_ready")
        pt_done = sem("pt_done")
        pt_ready = sem("pt_ready")
        pv_done = sem("pv_done")
        unit_out = sem("unit_out")
        tanh_ready = sem("tanh_ready")
        gated_ready = sem("gated_ready")
        gt_hi = sem("gt_hi")
        gt_lo = sem("gt_lo")
        moments_ready = sem("moments_ready")
        rstd_ready = sem("rstd_ready")
        pow_ready = sem("pow_ready")
        scaled = sem("scaled")
        rows_ready = sem("rows_ready")
        dve_step = sem("dve_step")
        act_step = sem("act_step")

        block = ctx.enter_context(nc.Block())

        @block.sync
        def _(sp):
            def slab(s, first=False):
                for j in range(PIECES):
                    if not (first and j < RING):
                        sp.wait_ge(lo_ready, PIECES * s + j - RING + 1)
                    sp.dma_start(raw[:, j % RING], w[s, :, j * PIECE_KT:(j + 1) * PIECE_KT, :]
                                 ).then_inc(w_landed[j % RING], 16)

            slab(0, first=True)
            with nc.Fori(1, SLABS, engines=(sp.engine,)) as s:
                slab(s)
            for t in range(T):
                for c in range(4):
                    sp.wait_ge(rows_ready, 4 * t + c + 1)
                    sp.dma_start(out[t * P:(t + 1) * P, c * COLS:(c + 1) * COLS],
                                 res[:, t, c * COLS:(c + 1) * COLS]).then_inc(out_landed, 16)
            sp.wait_ge(out_landed, 16 * 4 * T)

        @block.gpsimd
        def _(pool):
            nc.gpsimd.memset(power[:], -0.5).then_inc(pow_ready, 1)
            pool.wait_ge(pow_ready, 1)
            pool.wait_ge(moments_ready, 1)
            nc.gpsimd.tensor_tensor(rstd[:], centre[:], power[:], ALU.pow).then_inc(rstd_ready, 1)

        @block.tensor
        def _(pe):
            def slab(s, stationary, jobs=None, before=None, first=False, accs_by_vector=None):
                jobs = jobs or {}
                for j in range(PIECES):
                    if before:
                        before(j)
                    pe.wait_ge(lo_ready, PIECES * s + j + 1)
                    for t in range(T):
                        if j == 0 and not first:
                            if accs_by_vector is None:
                                pe.wait_ge(acc_free, T * (s - 1) + t + 1)
                            else:
                                pe.wait_ge(y_free, T * accs_by_vector + t + 1)
                        for k in range(j * PIECE_KT, (j + 1) * PIECE_KT):
                            for a, b in ((0, 0), (0, 1), (1, 0)):
                                mm = nc.tensor.matmul(
                                    acc[t][:], stationary[:, a, k, t * P:(t + 1) * P],
                                    split[:, j % RING, b, k % PIECE_KT, :],
                                    start=(k == 0 and a + b == 0), stop=(k == KT - 1 and a == 1))
                        if j == PIECES - 1 and t == 0:
                            mm.then_inc(first_done, 1)
                    mm.then_inc(piece_used, 1)
                    if j in jobs:
                        jobs[j]()

            def xposes(group, sources, wait=None):
                if wait:
                    pe.wait_ge(*wait)
                for i, source in enumerate(sources):
                    tr = nc.tensor.transpose(xpose[group % 2][:, i * P:(i + 1) * P], source, ident)
                tr.then_inc(xpose_done, 1)

            def scores(n, e, q_t, k_t, kind, free=True):
                if free:
                    pe.wait_ge(pt_ready, n - 1)
                o = score[e]
                if kind == "causal":
                    parts = ((0, o[:, 0:P], k_t[:, 0:P]), (1, o[:, P:3 * P], k_t))
                elif kind == "full":
                    parts = ((0, o[:, 0:S], k_t), (1, o[:, S:2 * S], k_t))
                else:
                    parts = ((0, o[:, 0:N_CMP], k_t), (1, o[:, 16:16 + N_CMP], k_t))
                for t, dst, k in parts:
                    mm = nc.tensor.matmul(dst, q_t[:, t * P:(t + 1) * P], k, start=True, stop=True)
                mm.then_inc(scores_done, 1)

            def probs_transpose(n, e, kind):
                pe.wait_ge(probs_ready, n + 1)
                if kind == "cmp":
                    for t in range(T):
                        tr = nc.tensor.transpose(score[e][0:N_CMP, t * P:(t + 1) * P],
                                                 probs[:, e, 16 * t:16 * t + N_CMP], ident)
                else:
                    for i in range(3 if kind == "causal" else 4):
                        tr = nc.tensor.transpose(score[e][:, i * P:(i + 1) * P],
                                                 probs[:, e, i * P:(i + 1) * P], ident)
                tr.then_inc(pt_done, 1)

            def mix(n, e, v, kind, free=True):
                pe.wait_ge(pt_ready, n + 1)
                if free:
                    pe.wait_ge(unit_out, n - 1)
                o, p_t = mixed[e], probs_t[:, e]
                if kind == "cmp":
                    for t in range(T):
                        mm = nc.tensor.matmul(o[:, t * P:(t + 1) * P], probs_t[0:N_CMP, e, t * P:(t + 1) * P],
                                              v, start=True, stop=True)
                else:
                    steps = ((0, 0, 0), (1, 1, 0), (1, 2, 1)) if kind == "causal" else \
                        ((0, 0, 0), (0, 1, 1), (1, 2, 0), (1, 3, 1))
                    for t, i, k in steps:
                        alone = kind == "causal" and t == 0
                        mm = nc.tensor.matmul(o[:, t * P:(t + 1) * P], p_t[:, i * P:(i + 1) * P], v(k),
                                              start=(k == 0), stop=(k == 1 or alone))
                mm.then_inc(pv_done, 1)

            def four(group, free):
                pe.wait_ge(con_landed, 16 * 5)
                pe.wait_ge(acc_free, T * (four_slab[group] + 1))
                for b in range(2):
                    xposes(group + b, [nat[:, t, (2 * b + i) * P:(2 * b + i + 1) * P]
                                       for i in range(2) for t in range(T)],
                           (xpose_out, group + b - 1) if free else None)

            four_slab = {G_MEMK: MEM_K, G_QMEM: Q_MEM, G_CMP: KV_CMP}

            def mem_quarter(j):
                if j % 2 == 0:
                    pe.wait_ge(stat_lo, j // 2 + 1)
            slab(MEM_K, b_hl, before=mem_quarter, first=True)
            slab(MEM_V, b_hl, {1: lambda: four(G_MEMK, False)})

            def x_quarter(j):
                if j % 2 == 0:
                    pe.wait_ge(stat_lo, 4 + j // 2 + 1)
            slab(Q_MEM, x_hl, before=x_quarter)

            def gate_logits():
                pe.wait_ge(wg_lo, 1)
                for t in range(T):
                    for k in range(KT):
                        for a, b in ((0, 0), (0, 1), (1, 0)):
                            mm = nc.tensor.matmul(
                                mixed[t][:, 0:HEADS * BRANCHES], x_hl[:, a, k, t * P:(t + 1) * P],
                                wg_hl[:, b, k, :], start=(k == 0 and a + b == 0), stop=(k == KT - 1 and a == 1))
                mm.then_inc(gates_done, 1)
            slab(KV_CMP, x_hl, {1: lambda: four(G_QMEM, True), 3: gate_logits})

            def mem_scores(pair):
                pe.wait_ge(xpose_out, G_QMEM + 2)
                for e in range(2):
                    n = 2 * pair + e
                    scores(n, e, mem_q_t[:, n], mem_k_t[:, n], "full", free=pair > 0)

            def mem_transpose(pair):
                for e in range(2):
                    probs_transpose(2 * pair + e, e, "full")

            def mem_mix(pair):
                if pair == 0:
                    pe.wait_ge(gates_tanh, 1)
                for e in range(2):
                    n = 2 * pair + e
                    mix(n, e, lambda k, n=n: mem_v[:, k, n, :], "full", free=pair > 0)

            slab(KV_SEL, x_hl, {1: lambda: four(G_CMP, True), 2: lambda: mem_scores(0),
                                3: lambda: mem_transpose(0), 4: lambda: (mem_mix(0), mem_scores(1)),
                                5: lambda: mem_transpose(1), 6: lambda: mem_mix(1)})

            def branch_keys(group, count):
                pe.wait_ge(roped, count)
                xposes(group, [rot[:, t, i, :] for i in range(2) for t in range(T)], (xpose_out, group - 1))
            slab(KV_WIN, x_hl, {2: lambda: branch_keys(G_SEL, 1)})

            def compress_hidden():
                pe.wait_ge(w1_landed, 32)
                pe.wait_ge(blocks_ready, 1)
                pe.wait_ge(unit_out, MEM_HEADS)
                for which, w1 in enumerate((w1k, w1v)):
                    for l in range(CMP_LEN):
                        mm = nc.tensor.matmul(mixed[which][:, 0:2 * N_CMP], w1[:, l, :],
                                              blocks[:, which, l], start=(l == 0), stop=(l == CMP_LEN - 1))
                mm.then_inc(hid_done, 1)

            def compress_out():
                pe.wait_ge(hid_ready, 1)
                nc.tensor.matmul(mixed[0][:, 0:2 * N_CMP], w2_sb[:, 0, :], hid[:, 0, :], start=True, stop=True)
                for g in range(2):
                    mm = nc.tensor.matmul(mixed[1][0:N_CMP, g * P:(g + 1) * P],
                                          hid[:, 1, g * N_CMP:(g + 1) * N_CMP], w2_sb[:, 1, :],
                                          start=True, stop=True)
                mm.then_inc(cmp_done, 1)
            slab(HEAD0, x_hl, {1: compress_hidden, 2: lambda: branch_keys(G_WIN, 2), 4: compress_out})

            with nc.Fori(HEAD0 + 1, HEAD0 + 1 + HEADS, engines=(pe.engine,)) as s:
                h = s - (HEAD0 + 1)
                g = h // GROUP
                group, unit = G_HEAD + 2 * h, U_HEAD + 4 * h

                def head_xposes():
                    pe.wait_ge(roped, 3 + h)
                    pe.wait_ge(xpose_out, group - 1)
                    for i, src in enumerate((nat[:, 0, 0:P], nat[:, 1, 0:P], rot[:, 0, 0, :], rot[:, 1, 0, :])):
                        tr = nc.tensor.transpose(xpose[0][:, i * P:(i + 1) * P], src, ident)
                    tr.then_inc(xpose_done, 1)
                    pe.wait_ge(xpose_out, group)
                    for i, src in enumerate((rot[:, 0, 1, :], rot[:, 1, 1, :], rot[:, 0, 2, :], rot[:, 1, 2, :])):
                        tr = nc.tensor.transpose(xpose[1][:, i * P:(i + 1) * P], src, ident)
                    tr.then_inc(xpose_done, 1)

                def nsa_scores():
                    pe.wait_ge(xpose_out, group + 2)
                    pe.wait_ge(cmp_ready, 1)
                    for e in range(2):
                        scores(unit + e, e, head_t[:, 1], nsa_k_t[:, e].rearrange("p g t -> p (g t)")[:, bass.ds(g * S, S)], "causal")

                def nsa_transpose():
                    for e in range(2):
                        probs_transpose(unit + e, e, "causal")

                def nsa_mix():
                    for e in range(2):
                        mix(unit + e, e, lambda k, e=e: nsa_v[:, e, k].rearrange("p g d -> p (g d)")[:, bass.ds(g * P, P)],
                            "causal")

                def rest_scores():
                    scores(unit + 2, 0, head_t[:, 2], head_t[:, 3], "causal")
                    scores(unit + 3, 1, head_t[:, 0],
                           cmp_k_t[:].rearrange("p g n -> p (g n)")[:, bass.ds(g * N_CMP, N_CMP)], "cmp")

                def rest_transpose():
                    probs_transpose(unit + 2, 0, "causal")
                    probs_transpose(unit + 3, 1, "cmp")

                def rest_mix():
                    mix(unit + 2, 0, lambda k: nat[:, k, 3 * P:4 * P], "causal")
                    mix(unit + 3, 1, cmp_v[:].rearrange("n g d -> n (g d)")[:, bass.ds(g * P, P)], "cmp")

                slab(s, x_hl, {1: head_xposes, 2: nsa_scores, 3: nsa_transpose,
                               4: lambda: (nsa_mix(), rest_scores()), 5: rest_transpose, 6: rest_mix})

            def gated_xposes(i, t, free):
                if t == 0:
                    pe.wait_ge(gated_ready, i + 1)
                if free:
                    pe.wait_ge(gt_lo, 2 * i + t - 1)
                for c in range(4):
                    tr = nc.tensor.transpose(xpose[t][:, c * P:(c + 1) * P], gated[:, t, c * P:(c + 1) * P], ident)
                tr.then_inc(xpose_done, 1)

            pe.wait_ge(xpose_out, G_Z)
            slab_jobs = lambda i, free: {2: lambda: gated_xposes(i, 0, free), 3: lambda: gated_xposes(i, 1, free)}
            slab(Z0 + 1, x_hl, slab_jobs(0, False))
            with nc.Fori(Z0 + 2, OUT0, engines=(pe.engine,)) as s:
                slab(s, x_hl, slab_jobs(s - (Z0 + 1), True))

            def gated_quarter(j):
                if j % 2 == 0:
                    pe.wait_ge(gt_lo, 2 * (j // 2) + 2)
            slab(OUT0, b_hl, slab_jobs(3, True), before=gated_quarter)
            with nc.Fori(OUT0 + 1, SLABS, engines=(pe.engine,)) as s:
                slab(s, b_hl, accs_by_vector=s - (OUT0 + 1))

        @block.scalar
        def _(act):
            def hi(s, j, first=False):
                act.wait_ge(w_landed[j % RING], 16 * (PIECES // RING * s + j // RING + 1))
                if not (first and j < RING):
                    act.wait_ge(piece_used, PIECES * s + j - RING + 1)
                nc.scalar.activation(split[:, j % RING, 0], raw[:, j % RING], ACT.Copy).then_inc(hi_ready, 1)

            def slab(s, jobs=None, first=False):
                for j in range(PIECES):
                    hi(s, j, first)
                    if jobs and j in jobs:
                        jobs[j]()

            def take(s, place):
                act.wait_ge(first_done, s + 1)
                nc.scalar.activation(place(0), acc[0][:], ACT.Copy).then_inc(acc_free, 1)
                act.wait_ge(piece_used, PIECES * (s + 1))
                nc.scalar.activation(place(1), acc[1][:], ACT.Copy).then_inc(acc_free, 1)

            def xpose_take(group, place):
                act.wait_ge(xpose_done, group + 1)
                nc.scalar.activation(place, xpose[group % 2][:], ACT.Copy).then_inc(xpose_out, 1)

            def four(group, place):
                for b in range(2):
                    xpose_take(group + b, place[:, 2 * b:2 * b + 2].rearrange("p a t -> p (a t)"))

            def exps(n, e, kind):
                act.wait_ge(max_ready, n + 1)
                src = score[e] if kind == "full" else probs[:, e]
                spans = {"causal": ((0, P), (P, 3 * P)), "full": ((0, S), (S, 2 * S)),
                         "cmp": ((0, N_CMP), (16, 16 + N_CMP))}[kind]
                for t, (lo, up) in enumerate(spans):
                    ex = nc.scalar.activation(probs[:, e, lo:up], src[:, lo:up], ACT.Exp, scale=SCALE,
                                              bias=shift[:, e, t:t + 1], accum_out=total[:, e, t:t + 1])
                ex.then_inc(probs_ready, 1)

            def pt_take(n, e, kind, free=True):
                act.wait_ge(pt_done, n + 1)
                if free:
                    act.wait_ge(pv_done, n - 1)
                rows, width = {"causal": (P, 3 * P), "full": (P, 4 * P), "cmp": (N_CMP, S)}[kind]
                nc.scalar.activation(probs_t[0:rows, e, 0:width], score[e][0:rows, 0:width], ACT.Copy
                                     ).then_inc(pt_ready, 1)

            def stat_quarter(raw_t, dst, c):
                ks = slice(4 * c, 4 * c + 4)
                nc.scalar.activation(dst[:, 0, ks, :], raw_t[:, ks, :], ACT.Copy).then_inc(stat_hi, 1)

            for c in range(4):
                act.dma_start(mem_raw[:, 4 * c:4 * c + 4, :], mem_t[:, 4 * c:4 * c + 4, :]).then_inc(mem_landed[c], 16)
            act.dma_start(con[:], consts[:, :]).then_inc(con_landed, 16)
            act.dma_start(pos_i[:], positions[:, :]).then_inc(con_landed, 16)
            act.dma_start(cpos[:], cmp_pos[:, :, :]).then_inc(con_landed, 16)
            act.dma_start(w2_sb[:], w2[:, :, :]).then_inc(con_landed, 16)
            act.dma_start(wg_raw[:], w_gate[:, :, :]).then_inc(con_landed, 16)
            act.dma_start(x_raw, x_t[:, :, :]).then_inc(x_landed, 16)

            for j in range(PIECES):
                if j % 2 == 0:
                    act.wait_ge(mem_landed[j // 2], 16)
                    stat_quarter(mem_raw, b_hl, j // 2)
                hi(MEM_K, j, first=True)

            def x_quarter(c):
                if c == 0:
                    act.wait_ge(x_landed, 16)
                stat_quarter(x_raw, x_hl, c)
            slab(MEM_V, {2: lambda: take(MEM_K, lambda t: nat[:, t, :]), 3: lambda: x_quarter(0),
                         4: lambda: (four(G_MEMK, mem_k_t), x_quarter(1)),
                         5: lambda: x_quarter(2), 6: lambda: x_quarter(3)})

            def load_w1():
                act.wait_ge(stat_lo, 8)
                act.dma_start(w1k, w1_k[:, :, :]).then_inc(w1_landed, 16)
                act.dma_start(w1v, w1_v[:, :, :]).then_inc(w1_landed, 16)

            def sine_tables():
                act.wait_ge(reduced, 2)
                nc.scalar.activation(sn[:], angle, ACT.Sin)
                nc.scalar.activation(cs[:], turns, ACT.Sin).then_inc(sines, 1)
            slab(Q_MEM, {1: load_w1, 2: lambda: take(MEM_V, lambda t: mem_v[:, t].rearrange("p h d -> p (h d)")),
                         5: sine_tables})

            def gate_split():
                act.wait_ge(con_landed, 16 * 5)
                nc.scalar.activation(wg_hl[:, 0], wg_raw[:], ACT.Copy).then_inc(wg_hi, 1)

            def gate_take():
                act.wait_ge(gates_done, 1)
                for t in range(T):
                    th = nc.scalar.activation(gates[:, t], mixed[t][:, 0:HEADS * BRANCHES], ACT.Tanh, scale=0.5)
                th.then_inc(gates_tanh, 1)
            slab(KV_CMP, {1: gate_split, 2: lambda: take(Q_MEM, lambda t: nat[:, t, :]),
                          4: lambda: four(G_QMEM, mem_q_t), 6: gate_take})

            def take_kv_cmp():
                take(KV_CMP, lambda t: nat[:, t, :])

            def units(fn, ns_kinds, **kw):
                for e, (n, kind) in enumerate(ns_kinds):
                    fn(n, e, kind, **kw)

            pair = lambda q: [(2 * q, "full"), (2 * q + 1, "full")]
            slab(KV_SEL, {2: take_kv_cmp, 4: lambda: (four(G_CMP, cmp_t), units(exps, pair(0))),
                          5: lambda: units(pt_take, pair(0), free=False),
                          6: lambda: units(exps, pair(1)), 7: lambda: units(pt_take, pair(1))})

            def take_branch(s, which):
                for t in range(T):
                    act.wait_ge(first_done, s + 1) if t == 0 else act.wait_ge(piece_used, PIECES * (s + 1))
                    nc.scalar.activation(nat[:, t, 0:2 * P], acc[t][:, 0:2 * P], ACT.Copy)
                    nc.scalar.activation(nsa_v[:, which, t].rearrange("p g d -> p (g d)"), acc[t][:, 2 * P:4 * P],
                                         ACT.Copy).then_inc(acc_free, 1)

            def branch_keys(group, which):
                xpose_take(group, nsa_k_t[:, which].rearrange("p g t -> p (g t)"))
            slab(KV_WIN, {2: lambda: take_branch(KV_SEL, 0), 5: lambda: branch_keys(G_SEL, 0)})

            def hid_tanhs():
                act.wait_ge(hid_done, 1)
                for which in range(2):
                    nc.scalar.activation(hid_tanh[:, which], mixed[which][:, 0:2 * N_CMP], ACT.Tanh, scale=0.5)
                    th = nc.scalar.activation(hid_in[:, which], mixed[which][:, 0:2 * N_CMP], ACT.Copy)
                th.then_inc(hid_taken, 1)

            def cmp_take():
                act.wait_ge(cmp_done, 1)
                nc.scalar.activation(cmp_k_t[:].rearrange("p g n -> p (g n)"), mixed[0][:, 0:2 * N_CMP], ACT.Copy)
                nc.scalar.activation(cmp_v[:].rearrange("n g d -> n (g d)"), mixed[1][0:N_CMP, 0:2 * P],
                                     ACT.Copy).then_inc(cmp_ready, 1)

            def load_res():
                act.wait_ge(hid_done, 1)
                act.dma_start(res, x[:, :, :]).then_inc(res_landed, 16)
            slab(HEAD0, {2: lambda: take_branch(KV_WIN, 1), 4: hid_tanhs,
                         5: lambda: branch_keys(G_WIN, 1), 7: lambda: (cmp_take(), load_res())})

            with nc.Fori(HEAD0 + 1, HEAD0 + 1 + HEADS, engines=(act.engine,)) as s:
                h = s - (HEAD0 + 1)
                group, unit = G_HEAD + 2 * h, U_HEAD + 4 * h
                nsa = [(unit, "causal"), (unit + 1, "causal")]
                rest = [(unit + 2, "causal"), (unit + 3, "cmp")]

                def take_head():
                    act.wait_ge(unit_out, unit)
                    take(s - 1, lambda t: nat[:, t, :])

                def take_head_xposes():
                    for b in range(2):
                        act.wait_ge(xpose_done, group + b + 1)
                        nc.scalar.activation(head_t[:, 2 * b:2 * b + 2].rearrange("p a t -> p (a t)"),
                                             xpose[b][:], ACT.Copy).then_inc(xpose_out, 1)
                slab(s, {2: take_head, 4: lambda: (take_head_xposes(), units(exps, nsa)),
                         5: lambda: units(pt_take, nsa), 6: lambda: units(exps, rest),
                         7: lambda: units(pt_take, rest)})

            def take_z(s, i, first=False):
                if not first:
                    act.wait_ge(gated_ready, i)
                take(s, lambda t: nat[:, t, :])
                act.wait_ge(acc_free, T * (s + 1))
                nc.scalar.activation(tanh_z, nat[:], ACT.Tanh, scale=0.5).then_inc(tanh_ready, 1)

            def gated_hi(i):
                for t in range(T):
                    act.wait_ge(xpose_done, G_Z + 2 * i + t + 1)
                    nc.scalar.activation(b_hl[:, 0, 4 * i:4 * i + 4, t * P:(t + 1) * P] if isinstance(i, int) else
                                         b_hl[:, 0, bass.ds(4 * i, 4), t * P:(t + 1) * P],
                                         xpose[t][:].rearrange("p (c q) -> p c q", c=4), ACT.Copy
                                         ).then_inc(gt_hi, 1)

            act.wait_ge(unit_out, UNITS)
            slab(Z0 + 1, {2: lambda: take_z(Z0, 0, first=True), 6: lambda: gated_hi(0)})
            with nc.Fori(Z0 + 2, OUT0, engines=(act.engine,)) as s:
                slab(s, {2: lambda: take_z(s - 1, s - (Z0 + 1)), 6: lambda: gated_hi(s - (Z0 + 1))})
            slab(OUT0, {2: lambda: take_z(OUT0 - 1, 3), 6: lambda: gated_hi(3)})

            def load_affine():
                act.wait_ge(gated_ready, 4)
                act.dma_start(gain_sb, gain.to_broadcast([P, D])).then_inc(affine_landed, 16)
                act.dma_start(bias_sb, bias.to_broadcast([P, D])).then_inc(affine_landed, 16)
            load_affine()
            with nc.Fori(OUT0 + 1, SLABS, engines=(act.engine,)) as s:
                slab(s)

            act.wait_ge(moments_ready, 2)
            for t in range(T):
                for c in range(4):
                    part = res[:, t, c * COLS:(c + 1) * COLS]
                    nc.scalar.activation(part, part, ACT.Identity, scale=rstd[:, t:t + 1],
                                         bias=centre[:, t:t + 1]).then_inc(scaled, 1)

        @block.vector
        def _(dve):
            own = Count(dve, dve_step)

            def lo(s, j):
                dve.wait_ge(hi_ready, PIECES * s + j + 1)
                nc.vector.tensor_tensor(split[:, j % RING, 1], raw[:, j % RING],
                                        split[:, j % RING, 0].bitcast(F32), ALU.subtract).then_inc(lo_ready, 1)

            def slab(s, jobs=None):
                for j in range(PIECES):
                    lo(s, j)
                    if jobs and j in jobs:
                        jobs[j]()

            def stat_quarter(raw_t, dst, c, n):
                ks = slice(4 * c, 4 * c + 4)
                dve.wait_ge(stat_hi, n + 1)
                nc.vector.tensor_tensor(dst[:, 1, ks, :], raw_t[:, ks, :], dst[:, 0, ks, :].bitcast(F32),
                                        ALU.subtract).then_inc(stat_lo, 1)

            for j in range(PIECES):
                if j % 2 == 0:
                    stat_quarter(mem_raw, b_hl, j // 2, j // 2)
                lo(MEM_K, j)

            x_quarter = lambda c: stat_quarter(x_raw, x_hl, c, 4 + c)
            slab(MEM_V, {3: lambda: x_quarter(0), 4: lambda: x_quarter(1), 5: lambda: x_quarter(2),
                         6: lambda: x_quarter(3)})

            def reduce_angles():
                half = P // 2
                dve.wait_ge(con_landed, 16 * 5)
                own.mark(nc.vector.tensor_copy(pos_f[:], pos_i[:]))
                own.wait()
                for t in range(T):
                    for i in range(2):
                        ins = nc.vector.tensor_scalar(angle[:, t, i * half:(i + 1) * half], con[:, C_INV:C_INV + half],
                                                      pos_f[:, t:t + 1], None, ALU.mult)
                own.mark(ins)
                own.wait()
                own.mark(nc.vector.tensor_copy(cs[:], angle))
                for i, quarter in ((0, 0.0), (1, 0.25)):
                    value = (angle, turns)[i]
                    own.wait()
                    own.mark(nc.vector.tensor_scalar(sn[:], cs[:], 0.15915494309189535, quarter, ALU.mult, ALU.add))
                    own.wait()
                    own.mark(nc.vector.tensor_scalar(sn[:], sn[:], ROUND, None, ALU.add))
                    own.wait()
                    own.mark(nc.vector.tensor_scalar(sn[:], sn[:], ROUND, None, ALU.subtract))
                    own.wait()
                    source = cs[:]
                    for part in TWO_PI:
                        own.mark(nc.vector.scalar_tensor_tensor(value, sn[:], -part, source, ALU.mult, ALU.add))
                        own.wait()
                        source = value
                    if i:
                        own.mark(nc.vector.tensor_scalar(value, value, 1.5707963267948966, None, ALU.add))
                        own.wait()
                    else:
                        for t in range(T):
                            ins = nc.vector.tensor_scalar(value[:, t, 0:half], value[:, t, 0:half], -1.0, None, ALU.mult)
                        own.mark(ins)
                        own.wait()
                    nc.vector.tensor_scalar(value, value, PI_BELOW, -PI_BELOW, ALU.min, ALU.max)\
                        .then_inc(reduced, 1)
            slab(Q_MEM, {3: reduce_angles})

            def gate_split():
                dve.wait_ge(wg_hi, 1)
                nc.vector.tensor_tensor(wg_hl[:, 1], wg_raw[:], wg_hl[:, 0].bitcast(F32), ALU.subtract)\
                    .then_inc(wg_lo, 1)

            def gate_finish():
                dve.wait_ge(gates_tanh, 1)
                nc.vector.tensor_scalar(gates[:], gates[:], 0.5, 0.5, ALU.mult, ALU.add).then_inc(gates_ready, 1)
            slab(KV_CMP, {1: gate_split, 7: gate_finish})

            def maxima(n, e, kind, free=True):
                dve.wait_ge(scores_done, n + 1)
                if free:
                    dve.wait_ge(pt_done, n - 1)
                nc.vector.memset(waiter[:], 0.0)
                if kind == "full":
                    for t in range(T):
                        ins = nc.vector.tensor_reduce(top[:, e, t:t + 1], score[e][:, t * S:(t + 1) * S], AX_X, ALU.max)
                else:
                    spans = ((0, P, C_MASK), (P, 3 * P, C_MASK + P)) if kind == "causal" else \
                        ((0, N_CMP, C_CMASK), (16, 16 + N_CMP, C_CMASK + 16))
                    for t, (a, b, m) in enumerate(spans):
                        ins = nc.vector.tensor_tensor_reduce(probs[:, e, a:b], score[e][:, a:b], con[:, m:m + b - a],
                                                             1.0, -3.0e38, ALU.add, ALU.max, top[:, e, t:t + 1])
                own.mark(ins)
                own.wait()
                nc.vector.tensor_scalar(shift[:, e], top[:, e], -1e20, -SCALE, ALU.max, ALU.mult).then_inc(max_ready, 1)

            def weights(n, e, gate=None, kind="causal"):
                dve.wait_ge(probs_ready, n + 1)
                if kind == "cmp":
                    own.mark(nc.vector.tensor_tensor(total[:, e], total[:, e], no_block, ALU.add))
                    own.wait()
                own.mark(nc.vector.reciprocal(weight[:, e], total[:, e]))
                own.wait()
                if gate is not None:
                    own.mark(nc.vector.tensor_tensor(weight[:, e], weight[:, e], gate, ALU.mult))
                    own.wait()

            def outputs(n, e, place, add):
                dve.wait_ge(pv_done, n + 1)
                for t in range(T):
                    if add:
                        ins = nc.vector.scalar_tensor_tensor(place(t), mixed[e][:, t * P:(t + 1) * P],
                                                             weight[:, e, t:t + 1], place(t), ALU.mult, ALU.add)
                    else:
                        ins = nc.vector.tensor_scalar(place(t), mixed[e][:, t * P:(t + 1) * P],
                                                      weight[:, e, t:t + 1], None, ALU.mult)
                ins.then_inc(unit_out, 1)

            def mem_maxima(pair):
                for e in range(2):
                    maxima(2 * pair + e, e, "full", free=pair > 0)

            def mem_outputs(pair):
                for e in range(2):
                    n = 2 * pair + e
                    weights(n, e)
                    outputs(n, e, lambda t, n=n: mem_v[:, t, n, :], False)

            slab(KV_SEL, {4: lambda: mem_maxima(0), 6: lambda: (mem_outputs(0), mem_maxima(1)),
                          7: lambda: mem_outputs(1)})

            def rope(s, count, turned_groups):
                half = P // 2
                dve.wait_ge(acc_free, T * (s + 1))
                dve.wait_ge(xpose_done, turned_groups)
                src = nat[:].rearrange("p t (h d) -> p t h d", d=P)[:, :, 0:count, :]
                dst, second = rot[:, :, 0:count, :], turned[:, :, 0:count, :]
                table = lambda tab, a, b: tab[:, :, a:b].unsqueeze(2).to_broadcast([P, T, count, b - a])
                nc.vector.tensor_tensor(dst, src, table(cs, 0, P), ALU.mult)
                nc.vector.tensor_tensor(second[:, :, :, 0:half], src[:, :, :, half:P], table(sn, 0, half), ALU.mult)
                own.mark(nc.vector.tensor_tensor(second[:, :, :, half:P], src[:, :, :, 0:half],
                                                 table(sn, half, P), ALU.mult))
                own.wait()
                nc.vector.tensor_tensor(dst, dst, second, ALU.add).then_inc(roped, 1)

            def make_blocks():
                dve.wait_ge(xpose_out, G_CMP + 2)
                for which in range(2):
                    for g in range(2):
                        rows = cmp_t[:, 2 * which + g].rearrange("p (m b) -> p b m", b=CMP_STRIDE)
                        for a in range(CMP_LEN // CMP_STRIDE):
                            ls = slice(a * CMP_STRIDE, (a + 1) * CMP_STRIDE)
                            ins = nc.vector.tensor_tensor(
                                blocks[:, which, ls, g, :], rows[:, :, a:a + N_CMP],
                                cpos[:, which, ls].unsqueeze(2).to_broadcast([P, CMP_STRIDE, N_CMP]), ALU.add)
                ins.then_inc(blocks_ready, 1)

            def rope_selected():
                dve.wait_ge(sines, 1)
                rope(KV_SEL, 2, G_SEL)
            slab(KV_WIN, {3: rope_selected, 5: make_blocks})

            def hidden_silu():
                dve.wait_ge(hid_taken, 1)
                own.mark(nc.vector.tensor_scalar(hid_tanh[:], hid_tanh[:], 0.5, 0.5, ALU.mult, ALU.add))
                own.wait()
                nc.vector.tensor_tensor(hid[:], hid_tanh[:], hid_in[:], ALU.mult).then_inc(hid_ready, 1)
            slab(HEAD0, {3: lambda: rope(KV_WIN, 2, G_WIN), 4: hidden_silu})

            with nc.Fori(HEAD0 + 1, HEAD0 + 1 + HEADS, engines=(dve.engine,)) as s:
                h = s - (HEAD0 + 1)
                unit = U_HEAD + 4 * h
                own.loop(h, 1 + 4 + 8)
                gate = lambda b: gates[:, :, bass.ds(h * BRANCHES + b, 1)].rearrange("p t o -> p (t o)")
                nsa_place = lambda t: heads[:, t, bass.ds(h * P + HEADS * P, P)]
                moba_place = lambda t: heads[:, t, bass.ds(h * P, P)]

                def nsa_maxima():
                    for e in range(2):
                        maxima(unit + e, e, "causal")

                def nsa_outputs():
                    dve.wait_ge(gates_ready, 1)
                    weights(unit, 0, gate(1))
                    outputs(unit, 0, nsa_place, False)
                    weights(unit + 1, 1, gate(2))
                    dve.wait_ge(unit_out, unit + 1)
                    outputs(unit + 1, 1, nsa_place, True)

                def rest_maxima():
                    maxima(unit + 2, 0, "causal")
                    maxima(unit + 3, 1, "cmp")

                def rest_outputs():
                    weights(unit + 2, 0)
                    outputs(unit + 2, 0, moba_place, False)
                    weights(unit + 3, 1, gate(0), "cmp")
                    dve.wait_ge(unit_out, unit + 3)
                    outputs(unit + 3, 1, nsa_place, True)

                slab(s, {3: lambda: rope(s - 1, 3, G_HEAD + 2 * h), 4: nsa_maxima,
                         6: lambda: (nsa_outputs(), rest_maxima()), 7: rest_outputs})
                own.end_loop(HEADS)

            def gate_heads(i, source):
                dve.wait_ge(tanh_ready, i + 1)
                dve.wait_ge(xpose_done, G_Z + 2 * i)
                own.mark(nc.vector.scalar_tensor_tensor(gated, tanh_z, 1.0, nat[:], ALU.add, ALU.mult))
                own.wait()
                nc.vector.scalar_tensor_tensor(gated, gated, 0.5, source, ALU.mult, ALU.mult).then_inc(gated_ready, 1)

            def gated_lo(i):
                for t in range(T):
                    dve.wait_ge(gt_hi, 2 * i + t + 1)
                    part = lambda b: b_hl[:, b, 4 * i:4 * i + 4, t * P:(t + 1) * P] if isinstance(i, int) else \
                        b_hl[:, b, bass.ds(4 * i, 4), t * P:(t + 1) * P]
                    nc.vector.tensor_tensor(part(1), xpose[t][:].rearrange("p (c q) -> p c q", c=4),
                                            part(0).bitcast(F32), ALU.subtract).then_inc(gt_lo, 1)

            slab(Z0 + 1, {3: lambda: gate_heads(0, heads[:, :, 0:COLS]), 6: lambda: gated_lo(0)})
            with nc.Fori(Z0 + 2, OUT0, engines=(dve.engine,)) as s:
                i = s - (Z0 + 1)
                own.loop(i - 1, 1)
                slab(s, {3: lambda: gate_heads(i, heads[:, :, bass.ds(i * COLS, COLS)]), 6: lambda: gated_lo(i)})
                own.end_loop(2)
            slab(OUT0, {3: lambda: gate_heads(3, mem_v[:].rearrange("p t h d -> p t (h d)")),
                        6: lambda: gated_lo(3)})

            def take_y(o):
                cols = slice(o * COLS, (o + 1) * COLS) if isinstance(o, int) else bass.ds(o * COLS, COLS)
                dve.wait_ge(first_done, OUT0 + 1 + o)
                for t in range(T):
                    if t:
                        dve.wait_ge(piece_used, PIECES * (OUT0 + 1) + PIECES * o)
                    nc.vector.scalar_tensor_tensor(res[:, t, cols], res[:, t, cols], ALPHA, acc[t][:],
                                                   ALU.mult, ALU.add).then_inc(y_free, 1)

            def statistics(o):
                at = slice(o, o + 1) if isinstance(o, int) else bass.ds(o, 1)
                cols = slice(o * COLS, (o + 1) * COLS) if isinstance(o, int) else bass.ds(o * COLS, COLS)
                dve.wait_ge(y_free, T * o + 2)
                for t in range(T):
                    ins = nc.vector.bn_stats(stats[:, t, at, :].rearrange("p o k -> p (o k)"), res[:, t, cols])
                return ins

            dve.wait_ge(res_landed, 16)
            with nc.Fori(OUT0 + 1, SLABS, engines=(dve.engine,)) as s:
                o = s - (OUT0 + 1)
                slab(s, {2: lambda: take_y(o), 3: lambda: statistics(o)})
            take_y(3)
            own.mark(statistics(3))
            own.wait()
            for t in range(T):
                ins = nc.vector.bn_aggr(moments[:, t, :], stats[:, t].rearrange("p o k -> p (o k)"))
            own.mark(ins)
            own.wait()
            nc.vector.tensor_scalar(centre[:], moments[:, :, 1], EPS, None, ALU.add).then_inc(moments_ready, 1)
            dve.wait_ge(rstd_ready, 1)
            nc.vector.scalar_tensor_tensor(centre[:], moments[:, :, 0], -1.0, rstd[:], ALU.mult, ALU.mult)\
                .then_inc(moments_ready, 1)
            dve.wait_ge(affine_landed, 32)
            for t in range(T):
                for c in range(4):
                    cols = slice(c * COLS, (c + 1) * COLS)
                    dve.wait_ge(scaled, 4 * t + c + 1)
                    own.mark(nc.vector.tensor_tensor(res[:, t, cols], res[:, t, cols], gain_sb[:, cols], ALU.mult))
                    own.wait()
                    nc.vector.tensor_tensor(res[:, t, cols], res[:, t, cols], bias_sb[:, cols], ALU.add)\
                        .then_inc(rows_ready, 1)


def _constants():
    import numpy as np
    c = np.zeros((P, C_ALL), np.float32)
    q, k = np.arange(P)[:, None], np.arange(P)[None, :]
    future = np.where(k > q, np.float32(-1e30), np.float32(0))
    c[:, C_MASK:C_MASK + P] = future
    c[:, C_MASK + 2 * P:C_MASK + 3 * P] = future
    last = np.arange(N_CMP) * CMP_STRIDE + CMP_LEN - 1
    for t in range(T):
        seen = last[None, :] <= q + t * P
        c[:, C_CMASK + 16 * t:C_CMASK + 16 * t + N_CMP] = np.where(seen, np.float32(0), np.float32(-1e30))
        c[:, C_NONE + t] = ~seen.any(axis=1)
    c[:, C_ID:C_ID + P] = np.eye(P, dtype=np.float32)
    half = P // 2
    c[:, C_INV:C_INV + half] = np.float32(10000.0) ** (-np.arange(half, dtype=np.float32) / half)
    return c


def kernel(**inputs):
    import numpy as np
    import concourse.bacc as bacc
    from concourse.bass_utils import run_bass_kernel_spmd

    a = {k: np.asarray(v) for k, v in inputs.items()}
    w_in, half = a["w_in"], HEADS * P
    q_m, k_m, v_m, q_n, kv_n = 0, half, 2 * half, 3 * half, 4 * half
    g_n = kv_n + 12 * P
    q_mem = g_n + HEADS * BRANCHES
    z = q_mem + MEM_HEADS * P
    head = lambda base, h: w_in[:, base + h * P:base + (h + 1) * P]
    columns = [a["w_mem_kv"], w_in[:, q_mem:z], w_in[:, kv_n:g_n]]
    for h in range(HEADS):
        columns += [head(q_n, h), head(q_m, h), head(k_m, h), head(v_m, h)]
    columns += [w_in[:, z:], a["w_out"]]
    tiled = lambda m: m.reshape(KT, P, -1).transpose(1, 0, 2)
    w = np.concatenate(columns, axis=1).reshape(KT, P, SLABS, COLS).transpose(2, 1, 0, 3)
    arrays = {
        "w": w,
        "x_t": tiled(a["x"][0].T),
        "mem_t": tiled(a["mem"][0].T),
        "x_rows": a["x"][0].reshape(T, P, D).transpose(1, 0, 2),
        "w_gate": tiled(w_in[:, g_n:q_mem]),
        "positions_t": a["positions"][0].reshape(T, P).T,
        "constants": _constants(),
        "cmp_pos": np.stack([a["cmp_pos_k"].T, a["cmp_pos_v"].T], axis=1),
        "w1_k": a["w_cmp1_k"].transpose(1, 0, 2),
        "w1_v": a["w_cmp1_v"].transpose(1, 0, 2),
        "w2": np.stack([a["w_cmp2_k"], a["w_cmp2_v"]], axis=1),
        "gain": a["ln_gain"].reshape(1, D),
        "bias": a["ln_bias"].reshape(1, D),
    }
    arrays = {k: np.ascontiguousarray(v) for k, v in arrays.items()}
    nc = bacc.Bacc("TRN2", target_bir_lowering=False, num_devices=1)
    args = [nc.dram_tensor(k, v.shape, mybir.dt.from_np(v.dtype), kind="ExternalInput").ap() for k, v in arrays.items()]
    out = nc.dram_tensor("out", (S, D), F32, kind="ExternalOutput").ap()
    build(nc, *args, out)
    r = run_bass_kernel_spmd(nc, [arrays], core_ids=[0])
    return r.results[0]["out"].reshape(1, S, D)
```

```python
from contextlib import ExitStack

import concourse.bass as bass
from concourse import mybir
from concourse.alu_op_type import AluOpType as ALU

F32 = mybir.dt.float32
F32R = mybir.dt.float32r
I32 = mybir.dt.int32
ACT = mybir.ActivationFunctionType
AX_X = mybir.AxisListType.X

P = 128
S = 256
T = S // P
D = 2048
KT = D // P
COLS = 512
HEADS = 6
GROUP = 3
BRANCHES = 3
MEM_HEADS = 4
N_CMP = (S - 32) // 16 + 1
CMP_LEN = 32
CMP_STRIDE = 16
CMP_PAD = 16
GATES = HEADS * BRANCHES
QUAD = 32
PIECE_KT = 2
PIECES = KT // PIECE_KT
RING = 4
WARM_UP = 10
SCALE = float(P) ** -0.5
ALPHA = 2.0 ** 0.25
EPS = 1e-5

MEM_K, MEM_V, Q_MEM, KV_CMP, KV_SEL, KV_WIN, HEAD0 = range(7)
Z0 = HEAD0 + HEADS
OUT0 = Z0 + D // COLS
SLABS = OUT0 + D // COLS

C_MASK = 0
C_CMASK = C_MASK + 3 * P
C_NONE = C_CMASK + 16 * T
C_ID = C_NONE + T
C_INV = C_ID + P
C_SUM4 = C_INV + P // 2
C_ALL = C_SUM4 + QUAD

TWO_PI = (201 / 2 ** 5, 253 / 2 ** 17, 170 / 2 ** 25, 3.968374e-09)
PI_BELOW = 3.1415925
ROUND = 12582912.0

G_MEMK, G_QMEM, G_CMP, G_SEL, G_WIN, G_HEAD = 0, 2, 4, 6, 7, 8
G_Z = G_HEAD + 2 * HEADS

U_HEAD = MEM_HEADS
UNITS = U_HEAD + 4 * HEADS


class Count:

    def __init__(self, engine, semaphore):
        self.engine, self.semaphore, self.base, self.n = engine, semaphore, 0, 0

    def mark(self, instruction):
        instruction.then_inc(self.semaphore, 1)
        self.n += 1

    def wait(self):
        self.engine.wait_ge(self.semaphore, self.base + self.n)

    def loop(self, turn, per_turn):
        self.entry, self.per_turn = self.base + self.n, per_turn
        self.base, self.n = self.entry + turn * per_turn, 0

    def end_loop(self, turns):
        assert self.n == self.per_turn, self.n
        self.base, self.n = self.entry + turns * self.per_turn, 0


def build(nc, w, x_t, mem_t, x, w_gate, positions, consts, cmp_pos, w1_k, w1_v, w2, gain, bias, out):
    with ExitStack() as ctx:
        def sb(name, shape, dt=F32):
            return ctx.enter_context(nc.sbuf_tensor(name, shape, dt))

        def bank(name):
            return ctx.enter_context(nc.psum_tensor(name, [P, 512], F32))

        def sem(name):
            return ctx.enter_context(nc.semaphore(name))

        raw = sb("raw", [P, RING, PIECE_KT, COLS])
        split = sb("split", [P, RING, 2, PIECE_KT, COLS], F32R)
        x_hl = sb("x_hl", [P, 2, KT, S], F32R)
        b_hl = sb("b_hl", [P, 2, KT, S], F32R)
        more_slots = x_hl[:].rearrange("p a k t -> p (a k t)").rearrange(
            "p (r b k c) -> p r b k c", r=RING, b=2, k=PIECE_KT)
        last_slot = lambda j: split[:, j] if j < RING else more_slots[:, j - RING]
        area_a = sb("area_a", [P, KT * S])
        area_b = sb("area_b", [P, KT * S])
        x_raw = area_a[:].rearrange("p (k t) -> p k t", k=KT)
        w1k = area_a[:].rearrange("p (l e) -> p l e", l=CMP_LEN)
        heads = area_a[:].rearrange("p (h t) -> p h t", t=S)
        gain_sb, bias_sb = area_a[:, 0:D], area_a[:, D:2 * D]
        mem_raw = area_b[:].rearrange("p (k t) -> p k t", k=KT)
        w1v = area_b[:].rearrange("p (l e) -> p l e", l=CMP_LEN)
        res = area_b[:].rearrange("p (t c) -> p t c", t=T)

        nat = sb("nat", [P, T, COLS])
        rot = sb("rot", [P, T, 3, P])
        turned = sb("turned", [P, T, 3, P])
        head_t = sb("head_t", [P, 4, S])
        cmp_t = head_t
        nsa_k_t = sb("nsa_k_t", [P, 2, 2, S])
        nsa_v = sb("nsa_v", [P, 2, T, 2, P])
        mem_k_t = sb("mem_k_t", [P, MEM_HEADS, S])
        mem_q_t = sb("mem_q_t", [P, MEM_HEADS, S])
        mem_v = sb("mem_v", [P, T, MEM_HEADS, P])
        area_c = sb("area_c", [P, 2048])
        blocks = area_c[:].rearrange("p (w l g n) -> p w l g n", w=2, l=CMP_LEN, g=2)
        tanh_z = area_c[:, 0:1024].rearrange("p (t c) -> p t c", t=T)
        gated = area_c[:, 0:1024].rearrange("p (h t) -> p h t", t=S)
        silu = area_c[:, 1024:2048].rearrange("p (t c) -> p t c", t=T)
        probs = sb("probs", [P, 2, COLS])
        probs_t = sb("probs_t", [P, 2, COLS])
        cs = sb("cs", [P, T, P])
        sn = sb("sn", [P, T, P])
        angle = probs_t[:, 0, 0:S].rearrange("p (t c) -> p t c", t=T)
        turns = probs_t[:, 1, 0:S].rearrange("p (t c) -> p t c", t=T)
        con = sb("con", [P, C_ALL])
        mask, ident = con[:, C_MASK:C_MASK + 3 * P], con[:, C_ID:C_ID + P]
        no_block = con[:, C_NONE:C_NONE + T]
        pos_i = sb("pos_i", [P, T], I32)
        pos_f = sb("pos_f", [P, T])
        cpos = sb("cpos", [P, 2, CMP_LEN])
        w2_sb = sb("w2_sb", [P, 2, P])
        partial = sb("partial", [P, 2, P])
        hid = sb("hid", [P, 2, 2 * CMP_PAD])
        hid_in = sb("hid_in", [P, 2, 2 * CMP_PAD])
        hid_tanh = sb("hid_tanh", [P, 2, 2 * CMP_PAD])
        cmp_k_t = sb("cmp_k_t", [P, 2, CMP_PAD])
        cmp_v = sb("cmp_v", [N_CMP, 2, P])
        wg = sb("wg", [P, KT, QUAD])
        logits_t = probs[:, 1, 0:S]
        gates = sb("gates", [P, T, GATES])
        waiter = sb("waiter", [P, 1])
        top = sb("top", [P, 2, T])
        shift = sb("shift", [P, 2, T])
        total = sb("total", [P, 2, T])
        weight = sb("weight", [P, 2, T])
        stats = sb("stats", [P, T, 4, 6])
        moments = sb("moments", [P, T, 2])
        rstd = sb("rstd", [P, T])
        power = sb("power", [P, T])
        start_up = sb("start_up", [P, 1])
        spread = sb("spread", [P, T])
        centre = sb("centre", [P, T])

        acc = [bank(f"acc{t}") for t in range(T)]
        score = [bank(f"score{e}") for e in range(2)]
        xpose = [bank(f"xpose{e}") for e in range(2)]
        mixed = [bank(f"mixed{e}") for e in range(2)]

        w_landed = [sem(f"w_landed{i}") for i in range(RING)]
        first_tile_landed = sem("first_tile_landed")
        first_tile_hi = sem("first_tile_hi")
        first_tile_lo = sem("first_tile_lo")
        mem_landed = [sem(f"mem_landed{i}") for i in range(PIECES)]
        x_landed = [sem(f"x_landed{i}") for i in range(4)]
        con_landed = sem("con_landed")
        small_landed = sem("small_landed")
        w1_landed = sem("w1_landed")
        res_landed = sem("res_landed")
        affine_landed = sem("affine_landed")
        out_landed = sem("out_landed")
        hi_ready = sem("hi_ready")
        lo_ready = sem("lo_ready")
        piece_used = sem("piece_used")
        first_done = sem("first_done")
        last_done = sem("last_done")
        acc_free = sem("acc_free")
        y_free = sem("y_free")
        stat_hi = sem("stat_hi")
        stat_lo = sem("stat_lo")
        logits_done = sem("logits_done")
        logits_taken = sem("logits_taken")
        gates_done = sem("gates_done")
        zeros_ready = sem("zeros_ready")
        zeroed = sem("zeroed")
        partial_done = sem("partial_done")
        partial_taken = sem("partial_taken")
        gates_tanh = sem("gates_tanh")
        gates_ready = sem("gates_ready")
        reduced = sem("reduced")
        sines = sem("sines")
        roped = sem("roped")
        xpose_done = sem("xpose_done")
        xpose_out = sem("xpose_out")
        blocks_ready = sem("blocks_ready")
        hid_done = sem("hid_done")
        hid_taken = sem("hid_taken")
        hid_ready = sem("hid_ready")
        cmp_done = sem("cmp_done")
        cmp_ready = sem("cmp_ready")
        scores_done = sem("scores_done")
        max_ready = sem("max_ready")
        exp_ready = sem("exp_ready")
        probs_ready = sem("probs_ready")
        pt_done = sem("pt_done")
        pt_ready = sem("pt_ready")
        pv_done = sem("pv_done")
        out_taken = sem("out_taken")
        tanh_ready = sem("tanh_ready")
        silu_ready = sem("silu_ready")
        gated_ready = sem("gated_ready")
        gt_hi = sem("gt_hi")
        gt_lo = sem("gt_lo")
        moments_ready = sem("moments_ready")
        rstd_ready = sem("rstd_ready")
        centre_ready = sem("centre_ready")
        pow_ready = sem("pow_ready")
        scaled = sem("scaled")
        rows_ready = sem("rows_ready")
        gain_done = sem("gain_done")
        last_rows_ready = sem("last_rows_ready")
        dve_step = sem("dve_step")

        block = ctx.enter_context(nc.Block())

        @block.sync
        def _(sp):
            def slab(s, first=False, before=None, after=None):
                for j in range(PIECES):
                    if before:
                        before(j)
                    if not (first and j < RING):
                        sp.wait_ge(lo_ready, PIECES * s + j - RING + 1)
                    if first and j == 0:
                        sp.dma_start(raw[:, 0, 0], w[0, :, 0, :]).then_inc(first_tile_landed, 16)
                        sp.dma_start(raw[:, 0, 1:], w[0, :, 1:PIECE_KT, :]).then_inc(w_landed[0], 16)
                        continue
                    sp.dma_start(raw[:, j % RING], w[s, :, j * PIECE_KT:(j + 1) * PIECE_KT, :]
                                 ).then_inc(w_landed[j % RING], 16)
                    if after:
                        after(j)

            def mem_part(j):
                ks = slice(PIECE_KT * j, PIECE_KT * (j + 1))
                sp.dma_start(mem_raw[:, ks, :], mem_t[:, ks, :]).then_inc(mem_landed[j], 16)

            def x_and_small(j):
                if j == 0:
                    sp.dma_start(con[:], consts[:, :]).then_inc(con_landed, 16)
                if j == PIECES - 1:
                    sp.dma_start(pos_i[:], positions[:, :]).then_inc(small_landed, 16)
                    sp.dma_start(cpos[:], cmp_pos[:, :, :]).then_inc(small_landed, 16)
                    sp.dma_start(w2_sb[:], w2[:, :, :]).then_inc(small_landed, 16)
                    sp.dma_start(wg[:], w_gate[:, :, :]).then_inc(small_landed, 16)
                if j < 4:
                    ks = slice(4 * j, 4 * (j + 1))
                    sp.dma_start(x_raw[:, ks, :], x_t[:, ks, :]).then_inc(x_landed[j], 16)

            def w1_part(w1, source):
                def part(j):
                    if w1 is w1k and j == 0:
                        sp.wait_ge(logits_done, 1)
                    ls = slice(CMP_LEN // PIECES * j, CMP_LEN // PIECES * (j + 1))
                    sp.dma_start(w1[:, ls, :], source[:, ls, :]).then_inc(w1_landed, 16)
                return part

            slab(MEM_K, first=True, before=mem_part)
            slab(MEM_V, after=x_and_small)
            slab(Q_MEM)
            sp.wait_ge(stat_lo, PIECES + 4)
            slab(KV_CMP, after=w1_part(w1k, w1_k))
            slab(KV_SEL, after=w1_part(w1v, w1_v))
            with nc.Fori(KV_WIN, SLABS, engines=(sp.engine,)) as s:
                slab(s)
            for t in range(T):
                for c in (0, 1, 3, 2):
                    sp.wait_ge(*((last_rows_ready, t + 1) if c == 3 else (rows_ready, 3 * t + c + 1)))
                    sp.dma_start(out[t * P:(t + 1) * P, c * COLS:(c + 1) * COLS],
                                 res[:, t, c * COLS:(c + 1) * COLS]).then_inc(out_landed, 16)
            sp.wait_ge(out_landed, 16 * 4 * T)

        @block.gpsimd
        def _(pool):
            nc.gpsimd.memset(power[:], -0.5).then_inc(pow_ready, 1)
            nc.gpsimd.memset(area_c[:], 0.0).then_inc(zeroed, 1)
            pool.wait_ge(pow_ready, 1)
            for t in range(T):
                pool.wait_ge(moments_ready, t + 1)
                nc.gpsimd.tensor_tensor(rstd[:, t:t + 1], spread[:, t:t + 1], power[:, t:t + 1], ALU.pow)\
                    .then_inc(rstd_ready, 1)
                part = res[:, t, 3 * COLS:]
                pool.wait_ge(scaled, t + 1)
                nc.gpsimd.tensor_tensor(part, part, gain_sb[:, 3 * COLS:], ALU.mult).then_inc(gain_done, 1)
                pool.wait_ge(gain_done, t + 1)
                nc.gpsimd.tensor_tensor(part, part, bias_sb[:, 3 * COLS:], ALU.add).then_inc(last_rows_ready, 1)

        @block.tensor
        def _(pe):
            def slab(s, stationary, jobs=None, before=None, first=False, accs_by_vector=None):
                jobs = jobs or {}
                for j in range(PIECES):
                    if before:
                        before(j)
                    if not (first and j == 0):
                        pe.wait_ge(lo_ready, PIECES * s + j + 1)
                    for t in range(T):
                        if j == 0 and not first:
                            if accs_by_vector is None:
                                pe.wait_ge(acc_free, T * (s - 1) + t + 1)
                            else:
                                pe.wait_ge(y_free, T * accs_by_vector + t + 1)
                        for k in range(j * PIECE_KT, (j + 1) * PIECE_KT):
                            if first and j == 0 and t == 0:
                                pe.wait_ge(*((first_tile_lo, 1) if k == 0 else (lo_ready, 1)))
                            for a, b in ((0, 0), (0, 1), (1, 0)):
                                mm = nc.tensor.matmul(
                                    acc[t][:], stationary[:, a, k, t * P:(t + 1) * P],
                                    split[:, j % RING, b, k % PIECE_KT, :],
                                    start=(k == 0 and a + b == 0), stop=(k == KT - 1 and a == 1))
                        if t == T - 1:
                            mm.then_inc(piece_used, 1)
                        elif j == PIECES - 1:
                            mm.then_inc(first_done, 1)
                        if j + t / 2 in jobs:
                            jobs[j + t / 2]()

            def xposes(group, sources, wait=None):
                if wait:
                    pe.wait_ge(*wait)
                for i, source in enumerate(sources):
                    tr = nc.tensor.transpose(xpose[group % 2][:, i * P:(i + 1) * P], source, ident)
                tr.then_inc(xpose_done, 1)

            def scores(n, e, q_t, k_t, kind, free=True):
                if free:
                    pe.wait_ge(pt_ready, n - 1)
                o = score[e]
                if kind == "causal":
                    parts = ((0, o[:, 0:P], k_t[:, 0:P]), (1, o[:, P:3 * P], k_t))
                elif kind == "full":
                    parts = ((0, o[:, 0:S], k_t), (1, o[:, S:2 * S], k_t))
                else:
                    parts = ((0, o[:, 0:N_CMP], k_t), (1, o[:, 16:16 + N_CMP], k_t))
                for t, dst, k in parts:
                    mm = nc.tensor.matmul(dst, q_t[:, t * P:(t + 1) * P], k, start=True, stop=True)
                mm.then_inc(scores_done, 1)

            def probs_transpose(n, e, kind):
                pe.wait_ge(probs_ready, n + 1)
                if kind == "cmp":
                    for t in range(T):
                        tr = nc.tensor.transpose(score[e][0:N_CMP, t * P:(t + 1) * P],
                                                 probs[:, e, 16 * t:16 * t + N_CMP], ident)
                else:
                    for to, i in enumerate((0, 1, 2) if kind == "causal" else (0, 2, 1, 3)):
                        tr = nc.tensor.transpose(score[e][:, to * P:(to + 1) * P],
                                                 probs[:, e, i * P:(i + 1) * P], ident)
                tr.then_inc(pt_done, 1)

            def mix(n, e, into, v, kind, start=True, stop=True):
                pe.wait_ge(pt_ready, n + 1)
                o = mixed[into]
                if kind == "cmp":
                    mm = nc.tensor.matmul(o[:, 0:S], v, probs_t[0:N_CMP, e, 0:S], start=start, stop=stop,
                                          skip_group_check=True)
                else:
                    late = P if kind == "causal" else 0
                    nc.tensor.matmul(o[:, 0:S], v(0), probs_t[:, e, 0:S], start=start, stop=False,
                                     skip_group_check=True)
                    mm = nc.tensor.matmul(o[:, late:S], v(1), probs_t[:, e, S:2 * S - late], start=False, stop=stop,
                                          skip_group_check=True)
                mm.then_inc(pv_done, 1)

            def four(group, free):
                pe.wait_ge(con_landed, 16)
                pe.wait_ge(acc_free, T * (four_slab[group] + 1))
                for b in range(2):
                    xposes(group + b, [nat[:, t, (2 * b + i) * P:(2 * b + i + 1) * P]
                                       for i in range(2) for t in range(T)],
                           (xpose_out, group + b - 1) if free else None)

            four_slab = {G_MEMK: MEM_K, G_QMEM: Q_MEM, G_CMP: KV_CMP}

            pe.wait_ge(zeros_ready, 1)
            for _ in range(WARM_UP):
                nc.tensor.matmul(score[0][:, 0:P], probs[:, 0, 0:P], probs[:, 0, 0:P], start=True, stop=True)

            slab(MEM_K, b_hl, before=lambda j: pe.wait_ge(stat_lo, j + 1), first=True)
            slab(MEM_V, b_hl, {1.5: lambda: four(G_MEMK, False)})

            def x_quarter(j):
                if j % 2 == 0:
                    pe.wait_ge(stat_lo, PIECES + j // 2 + 1)
            def gate_logits():
                pe.wait_ge(small_landed, 16 * 4)
                pe.wait_ge(stat_lo, PIECES + 4)
                for k in range(KT):
                    q = k % 4
                    mm = nc.tensor.matmul(mixed[0][QUAD * q:QUAD * (q + 1), 0:S], wg[:, k], x_raw[:, k, :],
                                          start=(k < 4), stop=(k >= KT - 4))
                mm.then_inc(logits_done, 1)

            def gate_sum():
                pe.wait_ge(logits_taken, 1)
                for t in range(T):
                    mm = nc.tensor.matmul(mixed[1][:, t * GATES:(t + 1) * GATES], logits_t[:, t * P:(t + 1) * P],
                                          con[:, C_SUM4:C_SUM4 + GATES], start=True, stop=True)
                mm.then_inc(gates_done, 1)
            slab(Q_MEM, x_hl, {0.5: gate_logits, 6.5: gate_sum}, before=x_quarter)
            slab(KV_CMP, x_hl, {1.5: lambda: four(G_QMEM, True)})

            def mem_scores(n):
                pe.wait_ge(xpose_out, G_QMEM + 2)
                scores(n, n % 2, mem_q_t[:, n], mem_k_t[:, n], "full", free=n > 1)

            def mem_mix(n):
                pe.wait_ge(gates_tanh, 1)
                if n > 1:
                    pe.wait_ge(out_taken, n - 1)
                mix(n, n % 2, n % 2, lambda k: mem_v[:, k, n, :], "full")

            mem_transpose = lambda n: probs_transpose(n, n % 2, "full")
            slab(KV_SEL, x_hl, {
                0.5: lambda: mem_scores(0), 1: lambda: mem_scores(1), 1.5: lambda: four(G_CMP, True),
                2: lambda: mem_transpose(0), 2.5: lambda: mem_transpose(1),
                3.5: lambda: (mem_mix(0), mem_scores(2)), 4: lambda: (mem_mix(1), mem_scores(3)),
                5: lambda: mem_transpose(2), 5.5: lambda: mem_transpose(3),
                6: lambda: mem_mix(2), 6.5: lambda: mem_mix(3)})

            def branch_keys(group, count):
                pe.wait_ge(roped, count)
                xposes(group, [rot[:, t, i, :] for i in range(2) for t in range(T)], (xpose_out, group - 1))
            slab(KV_WIN, x_hl, {2.5: lambda: branch_keys(G_SEL, 1)})

            def compress_hidden():
                pe.wait_ge(w1_landed, 16 * 2 * PIECES)
                pe.wait_ge(blocks_ready, 1)
                pe.wait_ge(out_taken, MEM_HEADS)
                for which, w1 in enumerate((w1k, w1v)):
                    for l in range(CMP_LEN):
                        q = l % 4
                        mm = nc.tensor.matmul(mixed[which][QUAD * q:QUAD * (q + 1), 0:P],
                                              blocks[:, which, l].rearrange("p g n -> p (g n)"), w1[:, l, :],
                                              start=(l < 4), stop=(l >= CMP_LEN - 4))
                mm.then_inc(partial_done, 1)

            def compress_sum():
                pe.wait_ge(partial_taken, 1)
                for which in range(2):
                    mm = nc.tensor.matmul(mixed[which][:, 0:2 * CMP_PAD], partial[:, which],
                                          con[:, C_SUM4:C_SUM4 + QUAD], start=True, stop=True)
                mm.then_inc(hid_done, 1)

            def compress_out():
                pe.wait_ge(hid_ready, 1)
                nc.tensor.matmul(mixed[0][:, 0:2 * CMP_PAD], w2_sb[:, 0, :], hid[:, 0, :], start=True, stop=True)
                for g in range(2):
                    mm = nc.tensor.matmul(mixed[1][0:N_CMP, g * P:(g + 1) * P],
                                          hid[:, 1, g * CMP_PAD:g * CMP_PAD + N_CMP], w2_sb[:, 1, :],
                                          start=True, stop=True)
                mm.then_inc(cmp_done, 1)
            slab(HEAD0, x_hl, {0.5: compress_hidden, 2.5: lambda: branch_keys(G_WIN, 2), 2: compress_sum,
                               4.5: compress_out})

            for g in range(2):
                with nc.Fori(HEAD0 + 1 + g * GROUP, HEAD0 + 1 + (g + 1) * GROUP, engines=(pe.engine,)) as s:
                    h = s - (HEAD0 + 1)
                    group, unit = G_HEAD + 2 * h, U_HEAD + 4 * h

                    def head_xposes():
                        pe.wait_ge(roped, 3 + h)
                        sources = (nat[:, 0, 0:P], nat[:, 1, 0:P], rot[:, 0, 0, :], rot[:, 1, 0, :],
                                   rot[:, 0, 1, :], rot[:, 1, 1, :], rot[:, 0, 2, :], rot[:, 1, 2, :])
                        for b in range(2):
                            pe.wait_ge(xpose_out, group + b - 1)
                            for i in range(4):
                                tr = nc.tensor.transpose(xpose[b][:, i * P:(i + 1) * P], sources[4 * b + i], ident)
                            tr.then_inc(xpose_done, 1)

                    def nsa_scores(e):
                        pe.wait_ge(xpose_out, group + 2)
                        scores(unit + e, e, head_t[:, 1], nsa_k_t[:, e, g], "causal")

                    def nsa_mix(e):
                        if e == 0:
                            pe.wait_ge(cmp_ready, 1)
                            pe.wait_ge(out_taken, MEM_HEADS + 2 * h)
                        mix(unit + e, e, 0, lambda k: nsa_v[:, e, k, g], "causal", start=(e == 0), stop=False)

                    def moba_scores():
                        scores(unit + 2, 0, head_t[:, 2], head_t[:, 3], "causal")

                    def cmp_scores():
                        scores(unit + 3, 1, head_t[:, 0], cmp_k_t[:, g, 0:N_CMP], "cmp")

                    def moba_mix():
                        mix(unit + 2, 0, 1, lambda k: nat[:, k, 3 * P:4 * P], "causal")

                    def cmp_mix():
                        mix(unit + 3, 1, 0, cmp_v[:, g], "cmp", start=False)

                    slab(s, x_hl, {
                        1.5: head_xposes,
                        2: lambda: nsa_scores(0), 2.5: lambda: nsa_scores(1),
                        3.5: lambda: probs_transpose(unit, 0, "causal"),
                        4: lambda: probs_transpose(unit + 1, 1, "causal"),
                        4.5: lambda: (nsa_mix(0), moba_scores()), 5: lambda: (nsa_mix(1), cmp_scores()),
                        6: lambda: (probs_transpose(unit + 2, 0, "causal"), probs_transpose(unit + 3, 1, "cmp")),
                        6.5: lambda: (moba_mix(), cmp_mix())})

            def silu_xposes(i, b, free):
                if b == 0:
                    pe.wait_ge(silu_ready, i + 1)
                if free:
                    pe.wait_ge(gated_ready, 2 * i + b - 1)
                for c in range(2):
                    for t in range(T):
                        tr = nc.tensor.transpose(xpose[b][:, (2 * c + t) * P:(2 * c + t + 1) * P],
                                                 silu[:, t, (2 * b + c) * P:(2 * b + c + 1) * P], ident)
                tr.then_inc(xpose_done, 1)

            pe.wait_ge(xpose_out, G_Z)
            slab_jobs = lambda i, free: {2.5: lambda: silu_xposes(i, 0, free), 3.5: lambda: silu_xposes(i, 1, free)}
            slab(Z0 + 1, x_hl, slab_jobs(0, False))
            with nc.Fori(Z0 + 2, OUT0, engines=(pe.engine,)) as s:
                slab(s, x_hl, slab_jobs(s - (Z0 + 1), True))

            def gated_quarter(j):
                if j % 2 == 0:
                    pe.wait_ge(gt_lo, 2 * (j // 2) + 2)
            slab(OUT0, b_hl, slab_jobs(3, True), before=gated_quarter)
            with nc.Fori(OUT0 + 1, SLABS - 1, engines=(pe.engine,)) as s:
                slab(s, b_hl, accs_by_vector=s - (OUT0 + 1))
            for t in range(T):
                pe.wait_ge(y_free, T * (SLABS - 2 - OUT0) + t + 1)
                for j in range(PIECES):
                    if t == 0:
                        pe.wait_ge(lo_ready, PIECES * (SLABS - 1) + j + 1)
                    for k in range(j * PIECE_KT, (j + 1) * PIECE_KT):
                        for a, b in ((0, 0), (0, 1), (1, 0)):
                            mm = nc.tensor.matmul(acc[t][:], b_hl[:, a, k, t * P:(t + 1) * P],
                                                  last_slot(j)[:, b, k % PIECE_KT, :],
                                                  start=(k == 0 and a + b == 0), stop=(k == KT - 1 and a == 1))
                mm.then_inc(last_done, 1)

        @block.scalar
        def _(act):
            def hi(s, j, first=False):
                act.wait_ge(w_landed[j % RING], 16 * (PIECES // RING * s + j // RING + 1))
                if not (first and j < RING):
                    act.wait_ge(piece_used, PIECES * s + j - RING + 1)
                nc.scalar.activation(split[:, j % RING, 0], raw[:, j % RING], ACT.Copy).then_inc(hi_ready, 1)

            def slab(s, jobs=None, first=False):
                for j in range(PIECES):
                    hi(s, j, first)
                    if jobs and j in jobs:
                        jobs[j]()

            def take(s, place):
                act.wait_ge(first_done, s + 1)
                nc.scalar.activation(place(0), acc[0][:], ACT.Copy).then_inc(acc_free, 1)
                act.wait_ge(piece_used, PIECES * (s + 1))
                nc.scalar.activation(place(1), acc[1][:], ACT.Copy).then_inc(acc_free, 1)

            def xpose_take(group, place):
                act.wait_ge(xpose_done, group + 1)
                nc.scalar.activation(place, xpose[group % 2][:], ACT.Copy).then_inc(xpose_out, 1)

            def four(group, place):
                for b in range(2):
                    xpose_take(group + b, place[:, 2 * b:2 * b + 2].rearrange("p a t -> p (a t)"))

            def exps(n, e, kind):
                act.wait_ge(max_ready, n + 1)
                src = score[e] if kind == "full" else probs[:, e]
                spans = {"causal": ((0, P), (P, 3 * P)), "full": ((0, S), (S, 2 * S)),
                         "cmp": ((0, N_CMP), (16, 16 + N_CMP))}[kind]
                for t, (lo, up) in enumerate(spans):
                    ex = nc.scalar.activation(probs[:, e, lo:up], src[:, lo:up], ACT.Exp, scale=SCALE,
                                              bias=shift[:, e, t:t + 1], accum_out=total[:, e, t:t + 1])
                ex.then_inc(exp_ready, 1)

            def pt_take(n, e, kind, free=True):
                act.wait_ge(pt_done, n + 1)
                if free:
                    act.wait_ge(pv_done, n - 1)
                rows, width = {"causal": (P, 3 * P), "full": (P, 4 * P), "cmp": (N_CMP, S)}[kind]
                nc.scalar.activation(probs_t[0:rows, e, 0:width], score[e][0:rows, 0:width], ACT.Copy
                                     ).then_inc(pt_ready, 1)

            def stat_part(raw_t, dst, c, width=4):
                ks = slice(width * c, width * (c + 1))
                nc.scalar.activation(dst[:, 0, ks, :], raw_t[:, ks, :], ACT.Copy).then_inc(stat_hi, 1)

            act.wait_ge(pow_ready, 1)
            nc.scalar.activation(start_up[:], power[:, 0:1], ACT.Copy)
            for j in range(PIECES):
                act.wait_ge(mem_landed[j], 16)
                stat_part(mem_raw, b_hl, j, PIECE_KT)
                if j == 0:
                    act.wait_ge(first_tile_landed, 16)
                    nc.scalar.activation(split[:, 0, 0, 0], raw[:, 0, 0], ACT.Copy).then_inc(first_tile_hi, 1)
                    act.wait_ge(w_landed[0], 16)
                    nc.scalar.activation(split[:, 0, 0, 1:], raw[:, 0, 1:], ACT.Copy).then_inc(hi_ready, 1)
                else:
                    hi(MEM_K, j, first=True)

            def x_quarter(c):
                act.wait_ge(x_landed[c], 16)
                stat_part(x_raw, x_hl, c)
            slab(MEM_V, {1: lambda: take(MEM_K, lambda t: nat[:, t, :]), 3: lambda: x_quarter(0),
                         4: lambda: (four(G_MEMK, mem_k_t), x_quarter(1)),
                         5: lambda: x_quarter(2), 6: lambda: x_quarter(3)})

            def sine_tables():
                act.wait_ge(reduced, 2)
                nc.scalar.activation(sn[:], angle, ACT.Sin)
                nc.scalar.activation(cs[:], turns, ACT.Sin).then_inc(sines, 1)
            def logits_take():
                act.wait_ge(logits_done, 1)
                nc.scalar.activation(logits_t, mixed[0][:, 0:S], ACT.Copy).then_inc(logits_taken, 1)

            slab(Q_MEM, {1: lambda: take(MEM_V, lambda t: mem_v[:, t].rearrange("p h d -> p (h d)")),
                         5: logits_take, 7: sine_tables})

            def gate_take():
                act.wait_ge(gates_done, 1)
                nc.scalar.activation(gates[:].rearrange("p t g -> p (t g)"), mixed[1][:, 0:T * GATES], ACT.Tanh,
                                     scale=0.5).then_inc(gates_tanh, 1)
            slab(KV_CMP, {0: gate_take, 1: lambda: take(Q_MEM, lambda t: nat[:, t, :]),
                          4: lambda: four(G_QMEM, mem_q_t)})

            def take_kv_cmp():
                take(KV_CMP, lambda t: nat[:, t, :])

            def units(fn, ns_kinds):
                for e, (n, kind) in enumerate(ns_kinds):
                    fn(n, e, kind)

            def unit(fn, n, **kw):
                fn(n, n % 2, "full", **kw)
            slab(KV_SEL, {1: take_kv_cmp, 3: lambda: (unit(exps, 0), unit(exps, 1)),
                          4: lambda: (four(G_CMP, cmp_t), unit(pt_take, 0, free=False), unit(pt_take, 1, free=False)),
                          6: lambda: (unit(exps, 2), unit(exps, 3)),
                          7: lambda: (unit(pt_take, 2), unit(pt_take, 3))})

            def take_branch(s, which):
                for t in range(T):
                    act.wait_ge(first_done, s + 1) if t == 0 else act.wait_ge(piece_used, PIECES * (s + 1))
                    nc.scalar.activation(nat[:, t, 0:2 * P], acc[t][:, 0:2 * P], ACT.Copy)
                    nc.scalar.activation(nsa_v[:, which, t].rearrange("p g d -> p (g d)"), acc[t][:, 2 * P:4 * P],
                                         ACT.Copy).then_inc(acc_free, 1)

            def branch_keys(group, which):
                xpose_take(group, nsa_k_t[:, which].rearrange("p g t -> p (g t)"))
            slab(KV_WIN, {1: lambda: take_branch(KV_SEL, 0), 5: lambda: branch_keys(G_SEL, 0)})

            def partial_take():
                act.wait_ge(partial_done, 1)
                for which in range(2):
                    cp = nc.scalar.activation(partial[:, which], mixed[which][:, 0:P], ACT.Copy)
                cp.then_inc(partial_taken, 1)

            def hid_tanhs():
                act.wait_ge(hid_done, 1)
                for which in range(2):
                    nc.scalar.activation(hid_tanh[:, which], mixed[which][:, 0:2 * CMP_PAD], ACT.Tanh, scale=0.5)
                    th = nc.scalar.activation(hid_in[:, which], mixed[which][:, 0:2 * CMP_PAD], ACT.Copy)
                th.then_inc(hid_taken, 1)

            def cmp_take():
                act.wait_ge(cmp_done, 1)
                nc.scalar.activation(cmp_k_t[:].rearrange("p g n -> p (g n)"), mixed[0][:, 0:2 * CMP_PAD], ACT.Copy)
                nc.scalar.activation(cmp_v[:].rearrange("n g d -> n (g d)"), mixed[1][0:N_CMP, 0:2 * P],
                                     ACT.Copy).then_inc(cmp_ready, 1)

            def load_res():
                act.wait_ge(hid_done, 1)
                act.dma_start(res, x[:, :, :]).then_inc(res_landed, 16)
            slab(HEAD0, {1: lambda: take_branch(KV_WIN, 1), 3: partial_take, 4: hid_tanhs,
                         5: lambda: branch_keys(G_WIN, 1), 7: lambda: (cmp_take(), load_res())})

            with nc.Fori(HEAD0 + 1, HEAD0 + 1 + HEADS, engines=(act.engine,)) as s:
                h = s - (HEAD0 + 1)
                group, unit = G_HEAD + 2 * h, U_HEAD + 4 * h
                nsa = [(unit, "causal"), (unit + 1, "causal")]
                rest = [(unit + 2, "causal"), (unit + 3, "cmp")]

                def take_head():
                    act.wait_ge(pv_done, unit)
                    take(s - 1, lambda t: nat[:, t, :])

                def take_head_xposes():
                    for b in range(2):
                        act.wait_ge(xpose_done, group + b + 1)
                        nc.scalar.activation(head_t[:, 2 * b:2 * b + 2].rearrange("p a t -> p (a t)"),
                                             xpose[b][:], ACT.Copy).then_inc(xpose_out, 1)

                slab(s, {1: take_head, 4: lambda: (take_head_xposes(), units(exps, nsa)),
                         5: lambda: units(pt_take, nsa), 6: lambda: units(exps, rest),
                         7: lambda: units(pt_take, rest)})

            def take_z(s, i, first=False):
                if not first:
                    act.wait_ge(gt_lo, 2 * i)
                take(s, lambda t: nat[:, t, :])
                act.wait_ge(acc_free, T * (s + 1))
                nc.scalar.activation(tanh_z, nat[:], ACT.Tanh, scale=0.5).then_inc(tanh_ready, 1)

            def gated_hi(i):
                for b in range(2):
                    act.wait_ge(gated_ready, 2 * i + b + 1)
                    nc.scalar.activation(b_hl[:, 0, bass.ds(4 * i + 2 * b, 2), :], gated[:, 2 * b:2 * b + 2, :],
                                         ACT.Copy).then_inc(gt_hi, 1)

            act.wait_ge(pv_done, UNITS)
            slab(Z0 + 1, {1: lambda: take_z(Z0, 0, first=True), 6: lambda: gated_hi(0)})
            with nc.Fori(Z0 + 2, OUT0, engines=(act.engine,)) as s:
                slab(s, {1: lambda: take_z(s - 1, s - (Z0 + 1)), 6: lambda: gated_hi(s - (Z0 + 1))})
            slab(OUT0, {1: lambda: take_z(OUT0 - 1, 3), 6: lambda: gated_hi(3)})

            def load_affine():
                act.wait_ge(gated_ready, 8)
                act.dma_start(gain_sb, gain.to_broadcast([P, D])).then_inc(affine_landed, 16)
                act.dma_start(bias_sb, bias.to_broadcast([P, D])).then_inc(affine_landed, 16)
            load_affine()
            with nc.Fori(OUT0 + 1, SLABS - 1, engines=(act.engine,)) as s:
                slab(s)
            last = SLABS - 1
            for j in range(PIECES):
                if j < RING:
                    hi(last, j)
                else:
                    act.wait_ge(w_landed[j % RING], 16 * (PIECES // RING * last + 2))
                    nc.scalar.activation(last_slot(j)[:, 0], raw[:, j % RING], ACT.Copy).then_inc(hi_ready, 1)

            for t in range(T):
                act.wait_ge(centre_ready, t + 1)
                part = res[:, t, 3 * COLS:]
                nc.scalar.activation(part, part, ACT.Identity, scale=rstd[:, t:t + 1],
                                     bias=centre[:, t:t + 1]).then_inc(scaled, 1)

        @block.vector
        def _(dve):
            own = Count(dve, dve_step)

            def lo(s, j):
                dve.wait_ge(hi_ready, PIECES * s + j + 1)
                nc.vector.tensor_tensor(split[:, j % RING, 1], raw[:, j % RING],
                                        split[:, j % RING, 0].bitcast(F32), ALU.subtract).then_inc(lo_ready, 1)

            def slab(s, jobs=None):
                for j in range(PIECES):
                    lo(s, j)
                    if jobs and j in jobs:
                        jobs[j]()

            def stat_part(raw_t, dst, c, n, width=4):
                ks = slice(width * c, width * (c + 1))
                dve.wait_ge(stat_hi, n + 1)
                nc.vector.tensor_tensor(dst[:, 1, ks, :], raw_t[:, ks, :], dst[:, 0, ks, :].bitcast(F32),
                                        ALU.subtract).then_inc(stat_lo, 1)

            nc.vector.memset(probs[:, 0, 0:P], 0.0).then_inc(zeros_ready, 1)
            for j in range(PIECES):
                stat_part(mem_raw, b_hl, j, j, PIECE_KT)
                if j == 0:
                    for ready, count, ks in ((first_tile_hi, first_tile_lo, slice(0, 1)),
                                             (hi_ready, lo_ready, slice(1, PIECE_KT))):
                        dve.wait_ge(ready, 1)
                        nc.vector.tensor_tensor(split[:, 0, 1, ks], raw[:, 0, ks], split[:, 0, 0, ks].bitcast(F32),
                                                ALU.subtract).then_inc(count, 1)
                else:
                    lo(MEM_K, j)

            x_quarter = lambda c: stat_part(x_raw, x_hl, c, PIECES + c)
            slab(MEM_V, {3: lambda: x_quarter(0), 4: lambda: x_quarter(1), 5: lambda: x_quarter(2),
                         6: lambda: x_quarter(3)})

            half = P // 2

            def make_angles():
                dve.wait_ge(con_landed, 16)
                dve.wait_ge(small_landed, 16 * 4)
                own.mark(nc.vector.tensor_copy(pos_f[:], pos_i[:]))
                own.wait()
                for t in range(T):
                    for i in range(2):
                        ins = nc.vector.tensor_scalar(cs[:, t, i * half:(i + 1) * half], con[:, C_INV:C_INV + half],
                                                      pos_f[:, t:t + 1], None, ALU.mult)
                own.mark(ins)

            def reduce_angles(i):
                value, quarter = ((angle, 0.0), (turns, 0.25))[i]
                own.wait()
                own.mark(nc.vector.tensor_scalar(sn[:], cs[:], 0.15915494309189535, quarter, ALU.mult, ALU.add))
                own.wait()
                own.mark(nc.vector.tensor_scalar(sn[:], sn[:], ROUND, None, ALU.add))
                own.wait()
                own.mark(nc.vector.tensor_scalar(sn[:], sn[:], ROUND, None, ALU.subtract))
                own.wait()
                source = cs[:]
                for part in TWO_PI:
                    own.mark(nc.vector.scalar_tensor_tensor(value, sn[:], -part, source, ALU.mult, ALU.add))
                    own.wait()
                    source = value
                if i:
                    own.mark(nc.vector.tensor_scalar(value, value, 1.5707963267948966, None, ALU.add))
                else:
                    for t in range(T):
                        ins = nc.vector.tensor_scalar(value[:, t, 0:half], value[:, t, 0:half], -1.0, None, ALU.mult)
                    own.mark(ins)
                own.wait()
                nc.vector.tensor_scalar(value, value, PI_BELOW, -PI_BELOW, ALU.min, ALU.max).then_inc(reduced, 1)
            slab(Q_MEM, {3: make_angles, 4: lambda: reduce_angles(0), 6: lambda: reduce_angles(1)})

            def gate_finish():
                dve.wait_ge(gates_tanh, 1)
                nc.vector.tensor_scalar(gates[:], gates[:], 0.5, 0.5, ALU.mult, ALU.add).then_inc(gates_ready, 1)
            slab(KV_CMP, {7: gate_finish})

            def maxima(n, e, kind, free=True):
                dve.wait_ge(scores_done, n + 1)
                if free:
                    dve.wait_ge(pt_done, n - 1)
                nc.vector.memset(waiter[:], 0.0)
                if kind == "full":
                    for t in range(T):
                        ins = nc.vector.tensor_reduce(top[:, e, t:t + 1], score[e][:, t * S:(t + 1) * S], AX_X, ALU.max)
                else:
                    spans = ((0, P, C_MASK), (P, 3 * P, C_MASK + P)) if kind == "causal" else \
                        ((0, N_CMP, C_CMASK), (16, 16 + N_CMP, C_CMASK + 16))
                    for t, (a, b, m) in enumerate(spans):
                        ins = nc.vector.tensor_tensor_reduce(probs[:, e, a:b], score[e][:, a:b], con[:, m:m + b - a],
                                                             1.0, -3.0e38, ALU.add, ALU.max, top[:, e, t:t + 1])
                own.mark(ins)
                own.wait()
                nc.vector.tensor_scalar(shift[:, e], top[:, e], -1e20, -SCALE, ALU.max, ALU.mult).then_inc(max_ready, 1)

            def weights(n, e, gate=None, kind="causal"):
                dve.wait_ge(exp_ready, n + 1)
                if kind == "cmp":
                    own.mark(nc.vector.tensor_tensor(total[:, e], total[:, e], no_block, ALU.add))
                    own.wait()
                own.mark(nc.vector.reciprocal(weight[:, e], total[:, e]))
                own.wait()
                if gate is not None:
                    own.mark(nc.vector.tensor_tensor(weight[:, e], weight[:, e], gate, ALU.mult))
                    own.wait()

            def normalise(n, e, kind):
                spans = {"causal": ((0, P), (P, 3 * P)), "full": ((0, S), (S, 2 * S)),
                         "cmp": ((0, N_CMP), (16, 16 + N_CMP))}[kind]
                for t, (a, b) in enumerate(spans):
                    ins = nc.vector.tensor_scalar(probs[:, e, a:b], probs[:, e, a:b], weight[:, e, t:t + 1], None,
                                                  ALU.mult)
                ins.then_inc(probs_ready, 1)

            def out_take(n, into, place):
                dve.wait_ge(pv_done, n + 1)
                nc.vector.tensor_copy(place, mixed[into][:, 0:S]).then_inc(out_taken, 1)

            def mem_pair(q):
                for e in range(2):
                    maxima(2 * q + e, e, "full", free=q > 0)
                for e in range(2):
                    weights(2 * q + e, e)
                    normalise(2 * q + e, e, "full")

            def mem_out(q):
                for e in range(2):
                    out_take(2 * q + e, e, mem_q_t[:, 2 * q + e])

            slab(KV_SEL, {3: lambda: mem_pair(0), 6: lambda: (mem_out(0), mem_pair(1)), 7: lambda: mem_out(1)})

            def rope(s, count, turned_groups):
                half = P // 2
                dve.wait_ge(acc_free, T * (s + 1))
                dve.wait_ge(xpose_done, turned_groups)
                src = nat[:].rearrange("p t (h d) -> p t h d", d=P)[:, :, 0:count, :]
                dst, second = rot[:, :, 0:count, :], turned[:, :, 0:count, :]
                table = lambda tab, a, b: tab[:, :, a:b].unsqueeze(2).to_broadcast([P, T, count, b - a])
                nc.vector.tensor_tensor(dst, src, table(cs, 0, P), ALU.mult)
                nc.vector.tensor_tensor(second[:, :, :, 0:half], src[:, :, :, half:P], table(sn, 0, half), ALU.mult)
                own.mark(nc.vector.tensor_tensor(second[:, :, :, half:P], src[:, :, :, 0:half],
                                                 table(sn, half, P), ALU.mult))
                own.wait()
                nc.vector.tensor_tensor(dst, dst, second, ALU.add).then_inc(roped, 1)

            def make_blocks():
                dve.wait_ge(xpose_out, G_CMP + 2)
                dve.wait_ge(zeroed, 1)
                for which in range(2):
                    for g in range(2):
                        rows = cmp_t[:, 2 * which + g].rearrange("p (m b) -> p b m", b=CMP_STRIDE)
                        for a in range(CMP_LEN // CMP_STRIDE):
                            ls = slice(a * CMP_STRIDE, (a + 1) * CMP_STRIDE)
                            ins = nc.vector.tensor_tensor(
                                blocks[:, which, ls, g, 0:N_CMP], rows[:, :, a:a + N_CMP],
                                cpos[:, which, ls].unsqueeze(2).to_broadcast([P, CMP_STRIDE, N_CMP]), ALU.add)
                ins.then_inc(blocks_ready, 1)

            def rope_selected():
                dve.wait_ge(sines, 1)
                rope(KV_SEL, 2, G_SEL)
            slab(KV_WIN, {2: rope_selected, 5: make_blocks})

            def hidden_silu():
                dve.wait_ge(hid_taken, 1)
                own.mark(nc.vector.tensor_scalar(hid_tanh[:], hid_tanh[:], 0.5, 0.5, ALU.mult, ALU.add))
                own.wait()
                nc.vector.tensor_tensor(hid[:], hid_tanh[:], hid_in[:], ALU.mult).then_inc(hid_ready, 1)
            slab(HEAD0, {2: lambda: rope(KV_WIN, 2, G_WIN), 5: hidden_silu})

            with nc.Fori(HEAD0 + 1, HEAD0 + 1 + HEADS, engines=(dve.engine,)) as s:
                h = s - (HEAD0 + 1)
                unit = U_HEAD + 4 * h
                own.loop(h, 1 + 4 + 8)
                gate = lambda b: gates[:, :, bass.ds(h * BRANCHES + b, 1)].rearrange("p t o -> p (t o)")

                def nsa_pair():
                    for e in range(2):
                        maxima(unit + e, e, "causal")
                    dve.wait_ge(gates_ready, 1)
                    for e in range(2):
                        weights(unit + e, e, gate(1 + e))
                        normalise(unit + e, e, "causal")

                def rest_pair():
                    maxima(unit + 2, 0, "causal")
                    maxima(unit + 3, 1, "cmp")
                    weights(unit + 2, 0)
                    normalise(unit + 2, 0, "causal")
                    weights(unit + 3, 1, gate(0), "cmp")
                    normalise(unit + 3, 1, "cmp")

                def heads_out():
                    out_take(unit + 2, 1, heads[:, bass.ds(h, 1), :].rearrange("p o t -> p (o t)"))
                    out_take(unit + 3, 0, heads[:, bass.ds(h + HEADS, 1), :].rearrange("p o t -> p (o t)"))

                slab(s, {1: lambda: rope(s - 1, 3, G_HEAD + 2 * h), 4: nsa_pair, 6: rest_pair, 7: heads_out})
                own.end_loop(HEADS)

            def make_silu(i):
                dve.wait_ge(tanh_ready, i + 1)
                nc.vector.scalar_tensor_tensor(silu, tanh_z, 1.0, nat[:], ALU.add, ALU.mult).then_inc(silu_ready, 1)

            def gate_heads(i, source):
                for b in range(2):
                    dve.wait_ge(xpose_done, G_Z + 2 * i + b + 1)
                    nc.vector.scalar_tensor_tensor(gated[:, 2 * b:2 * b + 2, :],
                                                   xpose[b][:].rearrange("p (c t) -> p c t", c=2), 0.5,
                                                   source(b), ALU.mult, ALU.mult).then_inc(gated_ready, 1)
                for b in range(2):
                    dve.wait_ge(gt_hi, 2 * i + b + 1)
                    part = lambda hl: b_hl[:, hl, bass.ds(4 * i + 2 * b, 2), :]
                    nc.vector.tensor_tensor(part(1), gated[:, 2 * b:2 * b + 2, :], part(0).bitcast(F32),
                                            ALU.subtract).then_inc(gt_lo, 1)

            z_jobs = lambda i, source: {3: lambda: make_silu(i), 6: lambda: gate_heads(i, source)}
            slab(Z0 + 1, z_jobs(0, lambda b: heads[:, 2 * b:2 * b + 2, :]))
            with nc.Fori(Z0 + 2, OUT0, engines=(dve.engine,)) as s:
                i = s - (Z0 + 1)
                slab(s, z_jobs(i, lambda b: heads[:, bass.ds(4 * i + 2 * b, 2), :]))
            slab(OUT0, z_jobs(3, lambda b: mem_q_t[:, 2 * b:2 * b + 2, :]))

            def statistics(o, t):
                return nc.vector.bn_stats(stats[:, t, bass.ds(o, 1), :].rearrange("p o k -> p (o k)"),
                                          res[:, t, bass.ds(o * COLS, COLS)])

            def take_y(o, t):
                cols = bass.ds(o * COLS, COLS)
                dve.wait_ge(*((piece_used, PIECES * (OUT0 + 1) + PIECES * o) if t else (first_done, OUT0 + 1 + o)))
                nc.vector.scalar_tensor_tensor(res[:, t, cols], res[:, t, cols], ALPHA, acc[t][:],
                                               ALU.mult, ALU.add).then_inc(y_free, 1)

            def slab_statistics(o):
                dve.wait_ge(y_free, T * o + 2)
                for t in range(T):
                    statistics(o, t)

            dve.wait_ge(res_landed, 16)
            with nc.Fori(OUT0 + 1, SLABS - 1, engines=(dve.engine,)) as s:
                o = s - (OUT0 + 1)
                slab(s, {1: lambda: (take_y(o, 0), take_y(o, 1)), 2: lambda: slab_statistics(o)})
            last = SLABS - 1
            for j in range(PIECES):
                if j < RING:
                    lo(last, j)
                else:
                    dve.wait_ge(hi_ready, PIECES * last + j + 1)
                    nc.vector.tensor_tensor(last_slot(j)[:, 1], raw[:, j % RING], last_slot(j)[:, 0].bitcast(F32),
                                            ALU.subtract).then_inc(lo_ready, 1)
                if j in (1, 2):
                    take_y(2, j - 1)
                if j == 7:
                    slab_statistics(2)
            dve.wait_ge(affine_landed, 32)
            for t in range(T):
                dve.wait_ge(last_done, t + 1)
                own.mark(nc.vector.scalar_tensor_tensor(res[:, t, 3 * COLS:], res[:, t, 3 * COLS:], ALPHA, acc[t][:],
                                                        ALU.mult, ALU.add))
                own.wait()
                own.mark(statistics(3, t))
                own.wait()
                own.mark(nc.vector.bn_aggr(moments[:, t, :], stats[:, t].rearrange("p o k -> p (o k)")))
                own.wait()
                nc.vector.tensor_scalar(spread[:, t:t + 1], moments[:, t, 1:2], EPS, None, ALU.add)\
                    .then_inc(moments_ready, 1)
                quarter = lambda c: slice(c * COLS, (c + 1) * COLS)
                for c in range(3):
                    ins = nc.vector.scalar_tensor_tensor(res[:, t, quarter(c)], res[:, t, quarter(c)],
                                                         moments[:, t, 0:1], gain_sb[:, quarter(c)],
                                                         ALU.subtract, ALU.mult)
                    if c == 0:
                        dve.wait_ge(rstd_ready, t + 1)
                        nc.vector.scalar_tensor_tensor(centre[:, t:t + 1], moments[:, t, 0:1], -1.0,
                                                       rstd[:, t:t + 1], ALU.mult, ALU.mult).then_inc(centre_ready, 1)
                own.mark(ins)
                own.wait()
                for c in range(3):
                    nc.vector.scalar_tensor_tensor(res[:, t, quarter(c)], res[:, t, quarter(c)], rstd[:, t:t + 1],
                                                   bias_sb[:, quarter(c)], ALU.mult, ALU.add).then_inc(rows_ready, 1)


def _constants():
    import numpy as np
    c = np.zeros((P, C_ALL), np.float32)
    q, k = np.arange(P)[:, None], np.arange(P)[None, :]
    future = np.where(k > q, np.float32(-1e30), np.float32(0))
    c[:, C_MASK:C_MASK + P] = future
    c[:, C_MASK + 2 * P:C_MASK + 3 * P] = future
    last = np.arange(N_CMP) * CMP_STRIDE + CMP_LEN - 1
    for t in range(T):
        seen = last[None, :] <= q + t * P
        c[:, C_CMASK + 16 * t:C_CMASK + 16 * t + N_CMP] = np.where(seen, np.float32(0), np.float32(-1e30))
        c[:, C_NONE + t] = ~seen.any(axis=1)
    c[:, C_ID:C_ID + P] = np.eye(P, dtype=np.float32)
    c[:, C_SUM4:C_SUM4 + QUAD] = np.tile(np.eye(QUAD, dtype=np.float32), (4, 1))
    half = P // 2
    c[:, C_INV:C_INV + half] = np.float32(10000.0) ** (-np.arange(half, dtype=np.float32) / half)
    return c


def kernel(**inputs):
    import numpy as np
    import concourse.bacc as bacc
    from concourse.bass_utils import run_bass_kernel_spmd

    a = {k: np.asarray(v) for k, v in inputs.items()}
    w_in, half = a["w_in"], HEADS * P
    q_m, k_m, v_m, q_n, kv_n = 0, half, 2 * half, 3 * half, 4 * half
    g_n = kv_n + 12 * P
    q_mem = g_n + GATES
    z = q_mem + MEM_HEADS * P
    head = lambda base, h: w_in[:, base + h * P:base + (h + 1) * P]
    columns = [a["w_mem_kv"], w_in[:, q_mem:z], w_in[:, kv_n:g_n]]
    for h in range(HEADS):
        columns += [head(q_n, h), head(q_m, h), head(k_m, h), head(v_m, h)]
    columns += [w_in[:, z:], a["w_out"]]
    tiled = lambda m: m.reshape(KT, P, -1).transpose(1, 0, 2)
    w = np.concatenate(columns, axis=1).reshape(KT, P, SLABS, COLS).transpose(2, 1, 0, 3)
    arrays = {
        "w": w,
        "x_t": tiled(a["x"][0].T),
        "mem_t": tiled(a["mem"][0].T),
        "x_rows": a["x"][0].reshape(T, P, D).transpose(1, 0, 2),
        "w_gate": np.pad(tiled(w_in[:, g_n:q_mem]), ((0, 0), (0, 0), (0, QUAD - GATES))),
        "positions_t": a["positions"][0].reshape(T, P).T,
        "constants": _constants(),
        "cmp_pos": np.stack([a["cmp_pos_k"].T, a["cmp_pos_v"].T], axis=1),
        "w1_k": a["w_cmp1_k"].transpose(1, 0, 2),
        "w1_v": a["w_cmp1_v"].transpose(1, 0, 2),
        "w2": np.stack([a["w_cmp2_k"], a["w_cmp2_v"]], axis=1),
        "gain": a["ln_gain"].reshape(1, D),
        "bias": a["ln_bias"].reshape(1, D),
    }
    arrays = {k: np.ascontiguousarray(v) for k, v in arrays.items()}
    nc = bacc.Bacc("TRN2", target_bir_lowering=False, num_devices=1)
    args = [nc.dram_tensor(k, v.shape, mybir.dt.from_np(v.dtype), kind="ExternalInput").ap() for k, v in arrays.items()]
    out = nc.dram_tensor("out", (S, D), F32, kind="ExternalOutput").ap()
    build(nc, *args, out)
    r = run_bass_kernel_spmd(nc, [arrays], core_ids=[0])
    return r.results[0]["out"].reshape(1, S, D)
```
